# Optimizing a Trainium2 kernel written in Bass

```python
import jax, jax.numpy as jnp
from jax import lax
import numpy as np

D_MODEL = 1024
BATCH = 1
SEQ = 128
DEPTH = 1
DEC_BATCH = 1
DEC_SEQ = 512
PAST_LEN = 128

GRID_W = 64
HEAD_DIM = 64
N_HEADS = 12
N_KV_HEADS = 4
GQA_GROUP = N_HEADS // N_KV_HEADS
ATTN_DIM = N_HEADS * HEAD_DIM
KV_DIM = N_KV_HEADS * HEAD_DIM
F_GROUPS = 4
F_HD = 64
F_DIM = F_GROUPS * F_HD
MIX_DIM = F_DIM + ATTN_DIM
IN_DIM = F_DIM + ATTN_DIM + 2 * KV_DIM
WINDOW = 128
Q_BLOCK = 128
ROPE_THETA = 10000.0
N_EXPERTS = 64
TOP_K = 8
N_EXPERT_GROUPS = 8
TOPK_GROUPS = 4
EXPERT_DIM = 256
SHARED_DIM = 256
ROUTED_SCALE = 2.5
MOE_BLOCK = 128
EPS = 1e-6

kernel_name = 'hybrid_fourier_swa_moe_diffusion_step'

def rms_norm(x, g):
    x32 = x.astype(jnp.float32)
    y = x32 * lax.rsqrt(jnp.mean(x32 * x32, axis=-1, keepdims=True) + EPS)
    return (y * g.astype(jnp.float32)).astype(x.dtype)

def modulation(c, w_mod, b_mod):
    m = jax.nn.silu(c) @ w_mod + b_mod
    return jnp.split(m, 6, axis=-1)

def modulate(x, shift, scale):
    return x * (1 + scale) + shift

def project(x, g, shift, scale, w_in):
    B, T = x.shape[:2]
    p = modulate(rms_norm(x, g), shift, scale) @ w_in
    u = p[..., :F_DIM].reshape(B, T, F_GROUPS, F_HD)
    q = p[..., F_DIM:F_DIM + ATTN_DIM].reshape(B, T, N_HEADS, HEAD_DIM)
    k = p[..., F_DIM + ATTN_DIM:F_DIM + ATTN_DIM + KV_DIM].reshape(B, T, N_KV_HEADS, HEAD_DIM)
    v = p[..., F_DIM + ATTN_DIM + KV_DIM:].reshape(B, T, N_KV_HEADS, HEAD_DIM)
    return u, q, k, v

def fourier_mixer(u, w_fourier):
    B, T = u.shape[:2]
    f = jnp.fft.fft2(u.astype(jnp.float32), axes=(1, 3), norm='ortho').real.astype(u.dtype)
    return jnp.einsum('btgc,gcd->btgd', f, w_fourier).reshape(B, T, F_DIM)

def axial_rope(x):
    T = x.shape[1]
    rows = T // GRID_W
    row = jnp.repeat(jnp.arange(rows), GRID_W)
    col = jnp.tile(jnp.arange(GRID_W), rows)
    n_freq = HEAD_DIM // 4
    inv = ROPE_THETA ** (-jnp.arange(n_freq, dtype=jnp.float32) / n_freq)
    half = HEAD_DIM // 2

    def rot(xa, pos):
        ang = pos.astype(jnp.float32)[:, None] * inv[None, :]
        c = jnp.cos(ang)[None, :, None, :]
        s = jnp.sin(ang)[None, :, None, :]
        x1, x2 = jnp.split(xa.astype(jnp.float32), 2, axis=-1)
        return jnp.concatenate([x1 * c - x2 * s, x2 * c + x1 * s], axis=-1)

    return jnp.concatenate([rot(x[..., :half], row), rot(x[..., half:], col)], axis=-1).astype(x.dtype)

def to_blocks(q):
    B, T = q.shape[:2]
    nb = T // Q_BLOCK
    return q.reshape(B, nb, Q_BLOCK, N_KV_HEADS, GQA_GROUP, HEAD_DIM).transpose(1, 0, 2, 3, 4, 5)

def from_blocks(o):
    nb, B = o.shape[:2]
    return o.transpose(1, 0, 2, 3, 4, 5).reshape(B, nb * Q_BLOCK, ATTN_DIM)

def sink_logits(sink, B):
    s = sink.astype(jnp.float32).reshape(N_KV_HEADS, GQA_GROUP)[None, :, :, None, None]
    return jnp.broadcast_to(s, (B, N_KV_HEADS, GQA_GROUP, Q_BLOCK, 1))

def context_attention(q, k, v, sink):
    B, S = q.shape[:2]
    scale = HEAD_DIM ** -0.5
    sink_b = sink_logits(sink, B)

    def block(qblk):
        s = jnp.einsum('bqkgd,bjkd->bkgqj', qblk, k).astype(jnp.float32) * scale
        prob = jax.nn.softmax(jnp.concatenate([s, sink_b], axis=-1), axis=-1).astype(v.dtype)
        return jnp.einsum('bkgqj,bjkd->bqkgd', prob[..., :S], v)

    return from_blocks(lax.map(block, to_blocks(q)))

def latent_attention(q, k, v, k_ctx, v_ctx, sink):
    B, T = q.shape[:2]
    C = k_ctx.shape[1]
    nb = T // Q_BLOCK
    kw_len = Q_BLOCK + 2 * WINDOW
    pad = ((0, 0), (WINDOW, WINDOW), (0, 0), (0, 0))
    kp = jnp.pad(k, pad)
    vp = jnp.pad(v, pad)
    scale = HEAD_DIM ** -0.5
    sink_b = sink_logits(sink, B)
    a = jnp.arange(Q_BLOCK)
    j = jnp.arange(kw_len)

    def block(args):
        i, qblk = args
        start = i * Q_BLOCK
        kw = lax.dynamic_slice_in_dim(kp, start, kw_len, axis=1)
        vw = lax.dynamic_slice_in_dim(vp, start, kw_len, axis=1)
        kpos = start - WINDOW + j
        qpos = start + a
        valid = (kpos >= 0)[None, :] & (kpos < T)[None, :] & (jnp.abs(kpos[None, :] - qpos[:, None]) <= WINDOW)
        s_w = jnp.einsum('bqkgd,bjkd->bkgqj', qblk, kw).astype(jnp.float32) * scale
        s_w = jnp.where(valid[None, None, None], s_w, -jnp.inf)
        s_c = jnp.einsum('bqkgd,bjkd->bkgqj', qblk, k_ctx).astype(jnp.float32) * scale
        prob = jax.nn.softmax(jnp.concatenate([s_w, s_c, sink_b], axis=-1), axis=-1).astype(v.dtype)
        o_w = jnp.einsum('bkgqj,bjkd->bqkgd', prob[..., :kw_len], vw)
        o_c = jnp.einsum('bkgqj,bjkd->bqkgd', prob[..., kw_len:kw_len + C], v_ctx)
        return o_w + o_c

    return from_blocks(lax.map(block, (jnp.arange(nb), to_blocks(q))))

def route(xf, w_router, router_bias):
    N = xf.shape[0]
    s = jax.nn.sigmoid((xf @ w_router).astype(jnp.float32))
    sc = s + router_bias.astype(jnp.float32)
    per_group = N_EXPERTS // N_EXPERT_GROUPS
    gscore = lax.top_k(sc.reshape(N, N_EXPERT_GROUPS, per_group), 2)[0].sum(-1)
    _, gidx = lax.top_k(gscore, TOPK_GROUPS)
    gmask = jax.nn.one_hot(gidx, N_EXPERT_GROUPS, dtype=jnp.float32).sum(1) > 0
    emask = jnp.repeat(gmask, per_group, axis=1)
    _, idx = lax.top_k(jnp.where(emask, sc, -jnp.inf), TOP_K)
    w = jnp.take_along_axis(s, idx, axis=-1)
    w = w / jnp.sum(w, axis=-1, keepdims=True) * ROUTED_SCALE
    return idx, w

def moe_ffn(h, w_router, router_bias, w_gate, w_up, w_down, ws_gate, ws_up, ws_down):
    B, T, D = h.shape
    xf = h.reshape(-1, D)
    N = xf.shape[0]
    idx, gates = route(xf, w_router, router_bias)
    NK = N * TOP_K
    flat_e = idx.reshape(-1)
    flat_tok = jnp.repeat(jnp.arange(N, dtype=jnp.int32), TOP_K)
    flat_g = gates.reshape(-1)
    order = jnp.argsort(flat_e)
    sorted_e = flat_e[order]
    counts = jnp.bincount(flat_e, length=N_EXPERTS)
    starts = jnp.cumsum(counts) - counts
    padded = (counts + MOE_BLOCK - 1) // MOE_BLOCK * MOE_BLOCK
    pad_ends = jnp.cumsum(padded)
    pad_starts = pad_ends - padded
    dest = pad_starts[sorted_e] + jnp.arange(NK) - starts[sorted_e]
    n_blocks = -(-NK // MOE_BLOCK) + N_EXPERTS
    R = n_blocks * MOE_BLOCK
    row_tok = jnp.full((R,), N, jnp.int32).at[dest].set(flat_tok[order])
    row_gate = jnp.zeros((R,), jnp.float32).at[dest].set(flat_g[order])
    block_e = jnp.minimum(jnp.searchsorted(pad_ends, jnp.arange(n_blocks) * MOE_BLOCK, side='right'), N_EXPERTS - 1)
    xpad = jnp.concatenate([xf, jnp.zeros((1, D), xf.dtype)], axis=0)

    def expert_block(args):
        tok, e = args
        xb = xpad[tok]
        hb = jax.nn.silu(xb @ w_gate[e]) * (xb @ w_up[e])
        return hb @ w_down[e]

    rows = lax.map(expert_block, (row_tok.reshape(n_blocks, MOE_BLOCK), block_e))
    routed = jax.ops.segment_sum(rows.reshape(R, D) * row_gate[:, None].astype(xf.dtype), row_tok, num_segments=N + 1)[:N]
    shared = (jax.nn.silu(xf @ ws_gate) * (xf @ ws_up)) @ ws_down
    return (routed + shared).reshape(B, T, D)

def ffn_sublayer(x, shift, scale, gate, p):
    h = modulate(rms_norm(x, p['norm2']), shift, scale)
    return x + gate * moe_ffn(h, p['w_router'], p['router_bias'], p['w_gate'], p['w_up'], p['w_down'],
                              p['ws_gate'], p['ws_up'], p['ws_down'])

def context_layer(x, c_ctx, p):
    sh1, sc1, g1, sh2, sc2, g2 = modulation(c_ctx[None, None, :], p['w_mod'], p['b_mod'])
    u, q, k, v = project(x, p['norm1'], sh1, sc1, p['w_in'])
    mix = jnp.concatenate([fourier_mixer(u, p['w_fourier']), context_attention(q, k, v, p['sink'])], axis=-1)
    x = x + g1 * (mix @ p['w_out'])
    return ffn_sublayer(x, sh2, sc2, g2, p), k, v

def latent_layer(x, c, k_ctx, v_ctx, p):
    sh1, sc1, g1, sh2, sc2, g2 = modulation(c[:, None, :], p['w_mod'], p['b_mod'])
    u, q, k, v = project(x, p['norm1'], sh1, sc1, p['w_in'])
    q = axial_rope(q)
    k = axial_rope(k)
    mix = jnp.concatenate([fourier_mixer(u, p['w_fourier']),
                           latent_attention(q, k, v, k_ctx, v_ctx, p['sink'])], axis=-1)
    x = x + g1 * (mix @ p['w_out'])
    return ffn_sublayer(x, sh2, sc2, g2, p)

def setup_inputs(seed: int = 0) -> dict:
    key = jax.random.key(seed)
    ks = jax.random.split(key, 24)
    f32 = jnp.float32

    def nrm(k, shape, scale):
        return jax.random.normal(k, shape, f32) * scale

    D = D_MODEL
    return {
        'x_prompt': nrm(ks[0], (BATCH, SEQ, D), 1.0),
        'x_sample': nrm(ks[1], (DEC_BATCH, DEC_SEQ, D), 1.0),
        'cache_k': nrm(ks[2], (DEC_BATCH, DEPTH, PAST_LEN, N_KV_HEADS, HEAD_DIM), 1.0),
        'cache_v': nrm(ks[3], (DEC_BATCH, DEPTH, PAST_LEN, N_KV_HEADS, HEAD_DIM), 1.0),
        'c': nrm(ks[4], (DEC_BATCH, D), 1.0),
        'c_ctx': nrm(ks[5], (D,), 1.0),
        'w_mod': nrm(ks[6], (DEPTH, D, 6 * D), 0.5 * D ** -0.5),
        'b_mod': nrm(ks[7], (DEPTH, 6 * D), 0.02),
        'norm1': 1.0 + nrm(ks[8], (DEPTH, D), 0.05),
        'w_in': nrm(ks[9], (DEPTH, D, IN_DIM), D ** -0.5),
        'w_fourier': nrm(ks[10], (DEPTH, F_GROUPS, F_HD, F_HD), F_HD ** -0.5),
        'sink': nrm(ks[11], (DEPTH, N_HEADS), 0.5),
        'w_out': nrm(ks[12], (DEPTH, MIX_DIM, D), MIX_DIM ** -0.5),
        'norm2': 1.0 + nrm(ks[13], (DEPTH, D), 0.05),
        'w_router': nrm(ks[14], (DEPTH, D, N_EXPERTS), D ** -0.5),
        'router_bias': nrm(ks[15], (DEPTH, N_EXPERTS), 0.01),
        'w_gate': nrm(ks[16], (DEPTH, N_EXPERTS, D, EXPERT_DIM), D ** -0.5),
        'w_up': nrm(ks[17], (DEPTH, N_EXPERTS, D, EXPERT_DIM), D ** -0.5),
        'w_down': nrm(ks[18], (DEPTH, N_EXPERTS, EXPERT_DIM, D), EXPERT_DIM ** -0.5),
        'ws_gate': nrm(ks[19], (DEPTH, D, SHARED_DIM), D ** -0.5),
        'ws_up': nrm(ks[20], (DEPTH, D, SHARED_DIM), D ** -0.5),
        'ws_down': nrm(ks[21], (DEPTH, SHARED_DIM, D), SHARED_DIM ** -0.5),
        'norm_f': 1.0 + nrm(ks[22], (D,), 0.05),
    }

def reference(x_prompt, x_sample, cache_k, cache_v, c, c_ctx, w_mod, b_mod, norm1, w_in, w_fourier, sink,
              w_out, norm2, w_router, router_bias, w_gate, w_up, w_down, ws_gate, ws_up, ws_down, norm_f):
    xp = x_prompt
    xs = x_sample
    new_ks = []
    new_vs = []
    for l in range(DEPTH):
        p = {'w_mod': w_mod[l], 'b_mod': b_mod[l], 'norm1': norm1[l], 'w_in': w_in[l],
             'w_fourier': w_fourier[l], 'sink': sink[l], 'w_out': w_out[l], 'norm2': norm2[l],
             'w_router': w_router[l], 'router_bias': router_bias[l], 'w_gate': w_gate[l],
             'w_up': w_up[l], 'w_down': w_down[l], 'ws_gate': ws_gate[l], 'ws_up': ws_up[l],
             'ws_down': ws_down[l]}
        xp, k_l, v_l = context_layer(xp, c_ctx, p)
        new_ks.append(k_l)
        new_vs.append(v_l)
        xs = latent_layer(xs, c, cache_k[:, l], cache_v[:, l], p)
    y_prompt = rms_norm(xp, norm_f)
    y_sample = rms_norm(xs, norm_f)
    new_k = jnp.stack(new_ks, axis=1)
    new_v = jnp.stack(new_vs, axis=1)
    return (y_prompt, y_sample, new_k, new_v)


_drawn_inputs = setup_inputs


def setup_inputs(seed=0):
    import zlib

    import numpy as np

    out = dict(_drawn_inputs(seed))
    spreads = {}
    factors = {'sink': 8.0}
    for name, (base, spread) in spreads.items():
        noise = np.random.default_rng([zlib.crc32(name.encode()), seed]).standard_normal(out[name].shape)
        drawn = base * np.exp(spread * noise) if base else spread * noise
        out[name] = __import__('jax').numpy.asarray(drawn.astype(out[name].dtype))
    for name, factor in factors.items():
        out[name] = (out[name] * factor).astype(out[name].dtype)
    return out
```

```python
from contextlib import ExitStack

import numpy as np
import concourse.bass as bass
from concourse import mybir

F32 = mybir.dt.float32
BF16 = mybir.dt.bfloat16
I32 = mybir.dt.int32
U32 = mybir.dt.uint32
ALU = mybir.AluOpType
ACT = mybir.ActivationFunctionType
AX = mybir.AxisListType.X

P = 128
D = 1024
KD = D // P
LAT = 4
T = 1 + LAT
NTOK = T * P
HD = 64
NH = 12
NKV = 4
FD = 256
PROJ = 1536
E = 64
TOPK = 8
F = 256
EPS = 1e-6
SCALE = HD ** -0.5
NEG = -1e30
ROUTED = 2.5
BLOCKS_MAX = E + (NTOK * TOPK) // (P + 1)
GROUPS = -(-BLOCKS_MAX // 4)
FIRST_GROUPS = E // 4
XBLK = 4 * GROUPS - E
NT = 4 * GROUPS + 2
NROW = NTOK * TOPK
SLOT = 6144

C_ID, C_ONE, C_IOTA, C_VT, C_N = 0, 128, 256, 384, 392
D_ROPE, D_DFT, D_C64, D_S64, D_U, D_ML, D_MR, D_N = 0, 512, 768, 896, 1024, 1152, 1280, 1408


def shape_constants():
    a = np.arange(P)
    keep = np.zeros((P, C_N), np.float32)
    keep[:, C_ID:C_ID + P] = np.eye(P)
    keep[:, C_ONE:C_ONE + P] = 1.0
    keep[:, C_IOTA:C_IOTA + P] = a[None, :]
    for t in range(T):
        keep[:, C_VT + t] = (t * P + a) * TOPK - NROW
    early = np.zeros((P, D_N), np.float64)
    inv = (10000.0 ** (-np.arange(16) / 16.0)).astype(np.float32)
    pos = np.arange(LAT * P)
    for half, where in ((0, pos // 64), (1, pos % 64)):
        ang = (where.astype(np.float32)[:, None] * inv[None, :]).astype(np.float32).astype(np.float64)
        c, s = np.cos(ang), np.sin(ang)
        for t in range(LAT):
            r = slice(t * P, (t + 1) * P)
            o = D_ROPE + t * 128 + half * 32
            early[:, o:o + 16], early[:, o + 16:o + 32] = c[r], c[r]
            early[:, o + 64:o + 80], early[:, o + 80:o + 96] = -s[r], s[r]
    w = 2 * np.pi * np.outer(a, a) / P
    early[:, D_DFT:D_DFT + 128] = np.cos(w) / P ** 0.5
    early[:, D_DFT + 128:D_DFT + 256] = np.sin(w) / P ** 0.5
    m = np.arange(HD)
    w = 2 * np.pi * np.outer(m, m) / HD
    for o, v in ((D_C64, np.cos(w) / 8), (D_S64, -np.sin(w) / 8)):
        early[0:64, o:o + 64] = v
        early[64:128, o + 64:o + 128] = v
    early[:, D_U:D_U + P] = a[:, None] < a[None, :]
    early[:, D_ML:D_ML + P] = np.where(a[None, :] >= a[:, None], 0.0, NEG)
    early[:, D_MR:D_MR + P] = np.where(a[None, :] <= a[:, None], 0.0, NEG)
    n = LAT * P
    w = 2 * np.pi * (np.outer(np.arange(n), np.arange(n)) % n) / n
    dft = np.stack([np.cos(w), np.sin(w)], 1) / n ** 0.5
    dft = dft.reshape(LAT, P, 2, n).transpose(1, 0, 2, 3).reshape(P, LAT * 2 * n)
    return keep, early.astype(np.float32), np.ascontiguousarray(dft.astype(np.float32))


def build(nc, x_prompt, x_sample, cache_k, cache_v, c, c_ctx, w_mod, b_mod, norm1, w_in, w_fourier, sink,
          w_out, norm2, w_router, router_bias, w_gate, w_up, w_down, ws_gate, ws_up, ws_down, norm_f,
          keep_c, early_c, dft_c, y_prompt, y_sample, new_k, new_v):
    ctx = ExitStack()
    with ctx:
        def sb(name, shape, dt=F32):
            return ctx.enter_context(nc.sbuf_tensor(name, shape, dt))

        def sem(name):
            return ctx.enter_context(nc.semaphore(name))

        h2_dram = nc.dram_tensor("h2_rows", (NTOK, D), F32, kind="Internal").ap()
        y_dram = nc.dram_tensor("expert_rows", (NROW, D), F32, kind="Internal").ap()

        ring = sb("ring", [P, 4 * SLOT])
        xs = sb("xs", [P, T, D])
        reg_h = sb("reg_h", [P, 5120])
        reg_p = sb("reg_p", [P, 7680])
        reg_b = sb("reg_b", [P, 6144])
        reg_y = sb("reg_y", [P, 2560])

        def view(reg, off, *dims):
            n = int(np.prod(dims))
            v = reg[:, off:off + n]
            if len(dims) == 2:
                v = v.rearrange("p (a b) -> p a b", a=dims[0])
            if len(dims) == 3:
                v = v.rearrange("p (a b c) -> p a b c", a=dims[0], b=dims[1])
            return v

        def slot(s):
            return s * SLOT

        def keys_of(t):
            if t == 0:
                return [5], P
            tiles = list(range(max(0, t - 2), min(LAT - 1, t) + 1)) + [4]
            return tiles, P * len(tiles)

        s3 = slot(3)
        xh = view(ring, s3, 2, D)
        prob = view(ring, s3 + 2048, 2, 512)
        prob_t = view(ring, s3 + 3072, 2, 512)
        qk = view(ring, s3 + 4096, 2, D)
        h1t = view(reg_h, 0, KD, NTOK)
        mix_t = view(reg_h, 0, KD, NTOK)
        u_sb = view(reg_p, 0, T, FD)
        v_sb = view(reg_p, 1280, T + 1, FD)
        q_t = view(reg_p, 2816, T, 6, P)
        on = view(reg_p, 6656, 2, 384)
        k_t = view(reg_b, 0, 2, 6 * P)
        y_cs = view(reg_b, 1536, 2, 512)
        rq = view(reg_b, 2560, D)
        rtmp = view(reg_b, 3584, D)
        kctx = view(reg_b, 4608, FD)
        early = view(reg_y, 0, D_N)
        w_bd = view(reg_y, 1408, 2, P)
        m_cs = view(reg_b, 4864, 2, 2, P)
        bc = view(reg_b, 0, 6, D)
        g2bc = view(reg_b, 0, 2, D)
        nfbc = view(reg_b, 2048, D)
        h2t = view(reg_p, 0, KD, NTOK)
        eq_ke = view(reg_p, 5120, TOPK, E)
        a_oh = view(reg_p, 5632, TOPK, P)
        eq_tmp = view(reg_p, 6656, TOPK, E)
        x2_tmp = view(reg_p, 5120, D)
        dg2 = view(reg_p, 7168, 4, P)
        up_sb = view(reg_b, 3072, 2, F)
        sh_out = view(reg_h, 2048, 2, D)
        h2row = view(reg_y, 0, 2, D)
        b_oh = view(reg_y, 0, TOPK, 2, NT)
        xg = view(reg_h, 0, 2, D)
        xg_t = view(reg_h, 2048, 2, KD * P)
        sg = view(reg_h, 4096, 2, F)
        hh = view(reg_h, 4608, 2, F)
        yb = view(reg_y, 0, 2, D)
        h_t = view(reg_y, 2048, 2, 2 * P)

        keep = sb("keep", [P, C_N])
        ident, ones, iota = keep[:, C_ID:C_ID + P], keep[:, C_ONE:C_ONE + P], keep[:, C_IOTA:C_IOTA + P]
        identb = sb("identb", [P, P], BF16)
        onesb = sb("onesb", [P, P], BF16)
        upper = sb("upper", [P, P], BF16)
        maskb = sb("maskb", [P, 2, P], BF16)
        cv = sb("cv", [P, 2, KD])
        cw = sb("cw", [P, 2, KD])
        silu_c = sb("silu_c", [P, 2, KD])
        bmod = sb("bmod", [P, 6, KD])
        nrm = sb("nrm", [P, 2, KD])
        mod = sb("mod", [P, 6, KD, 2])
        a1 = sb("a1", [P, KD, 2])
        a2 = sb("a2", [P, KD, 2])
        dg = view(ring, s3, 2, 4, P)
        nsink = sb("nsink", [P, NH])
        psink = sb("psink", [P, NH])
        ssq = sb("ssq", [P, 3 * T])
        rstd = sb("rstd", [P, 3 * T])
        mx = sb("mx", [P, 2])
        negm = sb("negm", [P, 2, NH])
        rsum = sb("rsum", [P, 2, NH])
        den = sb("den", [P, 2, 6])
        wr = view(reg_y, 2048, KD, E)
        rbias = sb("rbias", [P, E])
        sig = view(reg_b, 3584, T, E)
        sc = view(reg_b, 4640, E)
        g8 = view(reg_b, 4544, 8, 8)
        gsc = sb("gsc", [P, 8])
        top = sb("top", [P, 8])
        topi = sb("topi", [P, 8], U32)
        gif = sb("gif", [P, 8])
        geq = view(reg_b, 4608, 8, 4)
        gpen = sb("gpen", [P, 8])
        eif = sb("eif", [P, T, TOPK])
        gate = sb("gate", [P, T, TOPK])
        gsum = sb("gsum", [P, 2])
        maskm = sb("maskm", [P, T, E], BF16)
        xb = view(reg_b, 4704, E)
        xinc = view(reg_b, 4768, E)
        blk = view(reg_b, 3904, T, E)
        jmap = view(reg_b, 4224, T, E)
        pk = sb("pk", [P, 2, TOPK])
        vk = sb("vk", [P, TOPK])
        tripf = sb("tripf", [1, 16])
        tripn = sb("tripn", [1, 1])
        trip = sb("trip", [1, 1], I32)
        eidf = reg_b[0:1, 4832:4832 + NT]
        eid = sb("eid", [1, NT], I32)
        row_i = sb("row_i", [P, NT], U32)
        tok_i = sb("tok_i", [P, NT], U32)
        gate_s = sb("gate_s", [P, NT])
        tokc = sb("tokc", [P, 2], U32)
        rowc = sb("rowc", [P, 2], U32)

        bank = [ctx.enter_context(nc.psum_tensor(f"bank{i}", [P, 512], F32)) for i in range(8)]

        s_small = sem("small_inputs_in")
        s_x = sem("tokens_in")
        s_late = sem("attention_inputs_in")
        s_wf = sem("fourier_weights_in")
        s_late2 = sem("router_inputs_in")
        s_ring = [sem(f"ring_slot{i}_in") for i in range(4)]
        s_ac = sem("act_chain")
        s_dv = sem("dve_chain")
        s_cexp = sem("c_exp")
        s_silu = sem("silu_c_ready")
        s_modpe = sem("mod_chunk_done")
        s_modv = sem("mod_section_ready")
        s_ssq = sem("square_sums")
        s_var = sem("variance")
        s_std = sem("std")
        s_xh = sem("xhat_ready")
        s_tr = sem("xhat_transposed")
        s_h1a = sem("h1t_by_act")
        s_h1b = sem("h1t_by_dve")
        s_pa = sem("proj_even_group_done")
        s_pb = sem("proj_odd_group_done")
        s_ea = sem("proj_evacuated_by_act")
        s_eb = sem("proj_evacuated_by_dve")
        s_rot = sem("rotated")
        s_qk = sem("qk_transposed")
        s_qa = sem("qk_t_by_act")
        s_qb = sem("qk_t_by_dve")
        s_cst = sem("bf16_constants_ready")
        s_wbd0 = sem("w_blockdiag_cleared")
        s_m = sem("dft_w_done")
        s_me = sem("dft_w_ready")
        s_f = sem("fourier_pe")
        s_fa = sem("fourier_by_act")
        s_fb = sem("fourier_by_dve")
        s_s = sem("scores_done")
        s_nm = sem("neg_max_ready")
        s_ex = sem("probs_ready")
        s_pt = sem("probs_transposed")
        s_pta = sem("probs_t_by_act")
        s_ptb = sem("probs_t_by_dve")
        s_pvu = sem("pv_done")
        s_nk = sem("new_kv_out")
        s_se = sem("sink_exp_in")
        s_sx = sem("sink_exp_ready")
        s_on = sem("attn_out_normed")
        s_mt = sem("mix_transposed")
        s_mta = sem("mix_t_ready")
        s_dg = sem("diag_ready")
        s_bp = sem("broadcast_pe")
        s_ba = sem("broadcast_ready")
        s_op = sem("outproj_done")
        s_x2 = sem("outproj_read")
        s_x2r = sem("x2_ready")
        s_sq2 = sem("x2_squares")
        s_v2 = sem("x2_variance")
        s_st2 = sem("x2_std")
        s_h2 = sem("h2_rows_ready")
        s_h2o = [sem(f"h2_rows_out{i}") for i in range(2)]
        s_t2 = sem("h2_transposed")
        s_t2a = sem("h2t_by_act")
        s_t2b = sem("h2t_by_dve")
        s_r = sem("logits_done")
        s_re = sem("logit_exp_ready")
        s_rs = sem("sigmoid_ready")
        s_mm = sem("expert_mask_ready")
        s_pos = sem("positions_done")
        s_oh = sem("onehots_ready")
        s_tb = sem("table_tile_done")
        s_tab = sem("tables_ready")
        s_shg = sem("shared_gu_done")
        s_shs = sem("shared_silu_ready")
        s_shh = sem("shared_h_ready")
        s_sht = sem("shared_h_transposed")
        s_she = sem("shared_h_t_ready")
        s_shd = sem("shared_down_done")
        s_sho = sem("shared_out_copied")
        s_shm = sem("shared_gated")
        s_shx = sem("shared_added")
        s_xg = [sem(f"gathered{i}") for i in range(2)]
        s_idx = sem("pool_index_copied")
        s_pool = sem("pool_wait_passed")
        s_xt = sem("block_transposed")
        s_xa = sem("block_t_by_act")
        s_xb = sem("block_t_by_dve")
        s_g = sem("block_gate_up_done")
        s_sg = sem("block_silu_ready")
        s_h = sem("block_h_ready")
        s_ht = sem("block_h_transposed")
        s_he = sem("block_h_t_ready")
        s_y = sem("block_down_done")
        s_ya = sem("block_y_by_act")
        s_yb = sem("block_y_by_dve")
        s_yo = [sem(f"scattered{i}") for i in range(2)]
        s_g0 = sem("gather_buffers_cleared")
        s_row = [sem(f"token_rows_in{i}") for i in range(3)]
        s_fr = sem("token_rows_read")
        s_x3 = sem("x3_ready")
        s_sq3 = sem("x3_squares")
        s_v3 = sem("x3_variance")
        s_st3 = sem("x3_std")
        s_fin = sem("outputs_ready")
        s_out = sem("outputs_out")
        s_nf = sem("final_norm_in")
        block = ctx.enter_context(nc.Block())

        items = [("mod", 0, 0), ("mod", 1, 1), ("mod", 2, 2), ("mod", 3, 0), ("win", 0, 1), ("win", 1, 0)]
        items += [("mod", n, 2) for n in range(4, 12)] + [("dft", 0, 2), ("wout", 0, 0), ("wout", 1, 1)]
        uses = [sum(1 for it in items if it[2] == s) for s in range(4)]
        nth = {it[:2]: sum(1 for o in items[:n + 1] if o[2] == it[2]) for n, it in enumerate(items)}
        where = {it[:2]: it[2] for it in items}
        last_use = {"mod": lambda n: (s_modpe, n + 1), "win": lambda n: (s_pb, 2 * T), "dft": lambda n: (s_f, 7)}

        def arrived(eng, what, n):
            eng.wait_ge(s_ring[where[what, n]], 16 * nth[what, n])

        def item_slot(m):
            return (m + 2) % 4

        def experts_in(m_div, s):
            return 16 * uses[s] + 48 * (m_div + 1)

        def at_least(eng, s, value):
            if not isinstance(value, int) or value > 0:
                eng.wait_ge(s, value)

        def w_gu(s):
            return ring[:, slot(s):slot(s) + 4096].rearrange("p (w k f) -> p k w f", w=2, k=KD)

        def w_dn(s):
            return ring[:, slot(s) + 4096:slot(s) + SLOT].rearrange("p (k n) -> p k n", k=2)

        def load_expert(eng, s, gate_ap, up_ap, down_ap):
            o = slot(s)
            eng.dma_start(ring[:, o:o + 2048], gate_ap).then_inc(s_ring[s], 16)
            eng.dma_start(ring[:, o + 2048:o + 4096], up_ap).then_inc(s_ring[s], 16)
            eng.dma_start(ring[:, o + 4096:o + 6144], down_ap).then_inc(s_ring[s], 16)

        wg_v = w_gate.rearrange("l e (p k) f -> (l e) p (k f)", p=P)
        wu_v = w_up.rearrange("l e (p k) f -> (l e) p (k f)", p=P)
        wd_v = w_down.rearrange("l e (p k) n -> (l e) p (k n)", p=P)
        wmod_v = w_mod[0].rearrange("(p k) n -> p k n", p=P)
        win_v = w_in[0].rearrange("(p k) n -> p k n", p=P)
        wout_v = w_out[0].rearrange("(k p) n -> p k n", p=P)

        @block.sync
        def _(sp):
            before = {}
            for what, n, s in items:
                if s in before:
                    w, k = before[s]
                    sm, v = last_use[w](k)
                    sp.wait_ge(sm, v)
                before[s] = (what, n)
                o = slot(s)
                if what == "mod":
                    src = wmod_v[:, 4 * (n % 2):4 * (n % 2) + 4, (n // 2) * D:(n // 2 + 1) * D]
                    sp.dma_start(view(ring, o, 4, D), src).then_inc(s_ring[s], 16)
                elif what == "win":
                    sp.dma_start(view(ring, o, 4, PROJ), win_v[:, 4 * n:4 * n + 4, :]).then_inc(s_ring[s], 16)
                elif what == "dft":
                    sp.dma_start(ring[:, o:o + 4096], dft_c).then_inc(s_ring[s], 16)
                else:
                    sp.dma_start(view(ring, o, 4, D), wout_v[:, 4 * n:4 * n + 4, :]).then_inc(s_ring[s], 16)
            sp.wait_ge(s_f, 7)
            load_expert(sp, 2, ws_gate[0].rearrange("(p k) f -> p (k f)", p=P),
                        ws_up[0].rearrange("(p k) f -> p (k f)", p=P),
                        ws_down[0].rearrange("(p k) n -> p (k n)", p=P))
            sp.wait_ge(s_bp, 12)
            load_expert(sp, 3, wg_v[0], wu_v[0], wd_v[0])
            sp.wait_ge(s_op, 2 * T)
            load_expert(sp, 0, wg_v[1], wu_v[1], wd_v[1])
            load_expert(sp, 1, wg_v[2], wu_v[2], wd_v[2])
            sp.wait_ge(s_shd, T)
            load_expert(sp, 2, wg_v[3], wu_v[3], wd_v[3])
            sp.wait_ge(s_tab, 1)
            last_g = sp.value_load(trip[0:1, 0:1], min_val=FIRST_GROUPS - 1, max_val=GROUPS - 1)
            with sp.Fori(1, GROUPS) as i:
                with sp.If(i < last_g + 1):
                    for j in range(4):
                        e = sp.value_load(eid[0:1, bass.ds(i * 4 + j, 1)], min_val=0, max_val=E - 1)
                        sp.wait_ge(s_y, i * 4 + j - 3)
                        load_expert(sp, item_slot(j + 1), wg_v[bass.ds(e, 1)].rearrange("e p n -> (e p) n"),
                                    wu_v[bass.ds(e, 1)].rearrange("e p n -> (e p) n"),
                                    wd_v[bass.ds(e, 1)].rearrange("e p n -> (e p) n"))
            sp.wait_ge(s_y, last_g * 4 + 4)
            sp.wait_ge(s_yo[0], last_g * 32 + 32)
            sp.wait_ge(s_yo[1], last_g * 32 + 32)
            for t in range(T):
                if t >= 3:
                    sp.wait_ge(s_fr, t - 2)
                sp.dma_start(ring[:, (t % 3) * 8192:(t % 3 + 1) * 8192],
                             y_dram[t * P * TOPK:(t + 1) * P * TOPK, :].rearrange("(p k) d -> p (k d)", k=TOPK))\
                  .then_inc(s_row[t % 3], 16)
            for t in range(T):
                sp.wait_ge(s_fin, t + 1)
                dst = y_prompt[0] if t == 0 else y_sample[0, (t - 1) * P:t * P, :]
                sp.dma_start(dst, xs[:, t, :]).then_inc(s_out, 16)
            sp.wait_ge(s_out, 16 * T)
            sp.wait_ge(s_nk, 32)

        @block.gpsimd
        def _(pool):
            def shared_add(pool, t):
                pool.wait_ge(s_sho, t + 1)
                pool.tensor_tensor(sh_out[:, t % 2, :], sh_out[:, t % 2, :], g2bc[:, min(t, 1), :], ALU.mult).then_inc(s_shm, 1)
                pool.wait_ge(s_shm, t + 1)
                pool.tensor_tensor(xs[:, t, :], xs[:, t, :], sh_out[:, t % 2, :], ALU.add).then_inc(s_shx, 1)

            pool.memset(w_bd, 0.0).then_inc(s_wbd0, 1)
            pool.wait_ge(s_wbd0, 1)
            for g in range(4):
                h = 64 * (g % 2)
                pool.dma_start(w_bd[h:h + 64, g // 2, h:h + 64], w_fourier[0, g]).then_inc(s_wf, 16)
            pool.wait_ge(s_op, 2 * T)
            pool.memset(xg, 0.0).then_inc(s_g0, 1)
            pool.wait_ge(s_ba, 16)
            for t in range(T):
                pool.wait_ge(s_shs, t + 1)
                if t >= 2:
                    pool.wait_ge(s_sht, t - 1)
                pool.tensor_tensor(hh[:, t % 2, :], sg[:, t % 2, :], up_sb[:, t % 2, :], ALU.mult).then_inc(s_shh, 1)
                if t >= 1:
                    shared_add(pool, t - 1)
            shared_add(pool, T - 1)
            pool.wait_ge(s_tab, 1)
            for b in range(2):
                pool.tensor_copy(tokc[:, b:b + 1], tok_i[:, b:b + 1]).then_inc(s_idx, 1)
            pool.wait_ge(s_h2o[0], 48)
            pool.wait_ge(s_h2o[1], 32)
            pool.wait_ge(s_g0, 1)

            def gather(p):
                pool.indirect_dma_start(out=xg[:, p, :], out_offset=None, in_=h2_dram,
                                        in_offset=bass.IndirectOffsetOnAxis(ap=tokc[:, p:p + 1], axis=0),
                                        bounds_check=NTOK - 1, oob_is_err=False).then_inc(s_xg[p], 16)

            def scatter(c, p, wait_c):
                pool.wait_ge(s_ya, c + 1)
                pool.wait_ge(s_yb, c + 1)
                pool.wait_ge(s_idx, wait_c)
                pool.sem_inc(s_pool, 1)
                pool.indirect_dma_start(out=y_dram, out_offset=bass.IndirectOffsetOnAxis(ap=rowc[:, p:p + 1], axis=0),
                                        in_=yb[:, p, :], in_offset=None,
                                        bounds_check=NROW - 1, oob_is_err=False).then_inc(s_yo[p], 16)

            pool.wait_ge(s_idx, 2)
            gather(0)
            gather(1)

            def step(i, j):
                b, p = i * 4 + j, j % 2
                pool.wait_ge(s_xt, b + 1)
                pool.sem_inc(s_pool, 1)
                pool.tensor_copy(tokc[:, p:p + 1], tok_i[:, bass.ds(b + 2, 1)]).then_inc(s_idx, 1)
                at_least(pool, s_yo[p], i * 32 + 16 * (j // 2))
                pool.sem_inc(s_pool, 1)
                pool.tensor_copy(rowc[:, p:p + 1], row_i[:, bass.ds(b, 1)]).then_inc(s_idx, 1)
                pool.wait_ge(s_idx, b * 2 + 3)
                pool.sem_inc(s_pool, 1)
                gather(p)
                if not (isinstance(b, int) and b == 0):
                    scatter(b - 1, 1 - p, b * 2 + 2)

            last_g = pool.value_load(trip[0:1, 0:1], min_val=FIRST_GROUPS - 1, max_val=GROUPS - 1)
            for j in range(4):
                step(0, j)
            with pool.Fori(1, GROUPS) as i:
                with pool.If(i < last_g + 1):
                    for j in range(4):
                        step(i, j)
            scatter(last_g * 4 + 3, 1, last_g * 8 + 10)
            pool.wait_ge(s_xg[0], last_g * 32 + 48)
            pool.wait_ge(s_xg[1], last_g * 32 + 48)

        @block.scalar
        def _(act):
            n_chain = [0]

            def link(ins):
                n_chain[0] += 1
                ins.then_inc(s_ac, 1)
                act.wait_ge(s_ac, n_chain[0])

            act.dma_start(cv[:, 0, :], c_ctx.rearrange("(p k) -> p k", p=P)).then_inc(s_small, 16)
            act.dma_start(cv[:, 1, :], c[0].rearrange("(p k) -> p k", p=P)).then_inc(s_small, 16)
            act.dma_start(bmod[:], b_mod[0].rearrange("(s p k) -> p s k", s=6, p=P)).then_inc(s_small, 16)
            act.dma_start(nrm[:, 0, :], norm1[0].rearrange("(p k) -> p k", p=P)).then_inc(s_small, 16)
            act.dma_start(nrm[:, 1, :], norm2[0].rearrange("(p k) -> p k", p=P)).then_inc(s_small, 16)
            act.dma_start(keep[:], keep_c).then_inc(s_small, 16)
            act.dma_start(xs[:, 0, :], x_prompt[0]).then_inc(s_x, 16)
            act.dma_start(xs[:, 1:T, :], x_sample[0].rearrange("(t p) d -> p t d", p=P)).then_inc(s_x, 16)
            act.dma_start(early, early_c).then_inc(s_late, 16)
            act.dma_start(psink[:], sink.to_broadcast([P, NH])).then_inc(s_late, 16)
            act.dma_start(kctx, cache_k[0, 0].rearrange("s h d -> s (h d)")).then_inc(s_late, 16)
            act.dma_start(v_sb[:, T, :], cache_v[0, 0].rearrange("s h d -> s (h d)")).then_inc(s_late, 16)
            act.dma_start(wr[:], w_router[0].rearrange("(p k) e -> p k e", p=P)).then_inc(s_late2, 16)
            act.dma_start(rbias[:], router_bias.to_broadcast([P, E])).then_inc(s_late2, 16)

            act.wait_ge(s_small, 96)
            act.activation(cw[:], cv[:], ACT.Exp, scale=-1.0).then_inc(s_cexp, 1)
            act.wait_ge(s_x, 32)
            for t in range(T):
                last = act.activation(prob.rearrange("p a b -> p (a b)"), xs[:, t, :], ACT.Square,
                                      accum_out=ssq[:, t:t + 1])
                if t < T - 1:
                    link(last)
            last.then_inc(s_ssq, 1)
            act.wait_ge(s_var, 1)
            act.activation(rstd[:, 0:T], ssq[:, 0:T], ACT.Sqrt).then_inc(s_std, 1)

            def h1_half(t):
                act.wait_ge(s_tr, 2 * t + 1)
                if t == 0:
                    act.wait_ge(s_modv, 3)
                for k in range(4):
                    cond = min(t, 1)
                    last = act.activation(h1t[:, k, t * P:(t + 1) * P], bank[2][:, k * P:(k + 1) * P], ACT.Identity,
                                          scale=a1[:, k, cond:cond + 1], bias=mod[:, 0, k, cond:cond + 1])
                last.then_inc(s_h1a, 1)

            def q_out(t):
                act.wait_ge(s_qk, 2 * t + 1)
                act.copy(q_t[:, t, 0:4, :].rearrange("p a b -> p (a b)"), bank[6][:, :]).then_inc(s_qa, 1)

            h1_half(0)
            for t in range(T):
                if t + 1 < T:
                    h1_half(t + 1)
                act.wait_ge(s_pa, 2 * t + 1)
                if t >= 2:
                    act.wait_ge(s_rot, t - 2) if t > 2 else act.wait_ge(s_qk, 2)
                act.copy(qk[:, t % 2, 0:384], bank[4][:, 0:384]).then_inc(s_ea, 1)
                act.wait_ge(s_pa, 2 * t + 2)
                act.copy(u_sb[:, t, :], bank[4][:, 0:FD]).then_inc(s_ea, 1)
                if t >= 1:
                    q_out(t - 1)
                if t == 0:
                    act.wait_ge(s_eb, 2)
                    act.dma_start(new_k[0, 0].rearrange("s h d -> s (h d)"), qk[:, 0, 768:1024]).then_inc(s_nk, 16)
                    act.dma_start(new_v[0, 0].rearrange("s h d -> s (h d)"), v_sb[:, 0, :]).then_inc(s_nk, 16)

            q_out(T - 1)
            act.wait_ge(s_m, 1)
            act.copy(m_cs.rearrange("p a b c -> p (a b c)"), bank[0][:, :]).then_inc(s_me, 1)
            n = 0
            for cc in range(2):
                for w0, wn in ((0, P), (P, 512)):
                    act.wait_ge(s_f, 1 + 2 * n)
                    act.copy(y_cs[:, 0, 0:wn], bank[0][:, 0:wn]).then_inc(s_fa, 1)
                    act.wait_ge(s_f, 2 + 2 * n)
                    act.copy(mix_t[:, cc, w0:w0 + wn], bank[2][:, 0:wn]).then_inc(s_fa, 1)
                    n += 1

            units = [(t, h) for t in range(T) for h in range(NH)]

            def exps(u):
                t, h = units[u]
                n_keys = keys_of(t)[1]
                act.wait_ge(s_nm, u + 1)
                if u >= 2:
                    act.wait_ge(s_pt, u - 1)
                act.activation(prob[:, u % 2, 0:n_keys], bank[u % 3][:, 0:n_keys], ACT.Exp, scale=SCALE,
                               bias=negm[:, t % 2, h:h + 1], accum_out=rsum[:, t % 2, h:h + 1]).then_inc(s_ex, 1)

            def half_tile(n):
                t, g = divmod(n, 2)
                act.wait_ge(s_se, n + 1)
                act.activation(den[:, n % 2, :], den[:, n % 2, :], ACT.Exp).then_inc(s_sx, 1)

            def mix_half(n):
                t, g = divmod(n, 2)
                act.wait_ge(s_mt, n + 1)
                act.copy(mix_t[:, 2 + 3 * g:5 + 3 * g, t * P:(t + 1) * P],
                         bank[7][:, 0:384].rearrange("p (a b) -> p a b", a=3)).then_inc(s_mta, 1)

            exps(0)
            exps(1)
            for u in range(len(units)):
                if u % 2:
                    act.wait_ge(s_pt, u + 1)
                    n_keys = keys_of(units[u][0])[1]
                    if u >= 2:
                        act.wait_ge(s_pvu, u - 1)
                    act.copy(prob_t[:, 1, 0:n_keys], bank[4][:, 0:n_keys]).then_inc(s_pta, 1)
                if u + 2 < len(units):
                    exps(u + 2)
                if u % 6 == 0 and u:
                    half_tile(u // 6 - 1)
                if u % 6 == 3 and u > 6:
                    mix_half(u // 6 - 1)
            half_tile(9)
            mix_half(9)

            for v in range(6):
                for hf in range(2):
                    n = 2 * v + hf
                    act.wait_ge(s_bp, n + 1)
                    act.copy(bc[:, v, :].rearrange("p (q k) -> p k q", k=KD)[:, 4 * hf:4 * hf + 4, :],
                             bank[n % 2][:, :].rearrange("p (k q) -> p k q", k=4)).then_inc(s_ba, 1)

            def norm2_of(t):
                act.wait_ge(s_x2r, t + 1)
                act.activation(h2row[:, t % 2, :], xs[:, t, :], ACT.Square,
                               accum_out=ssq[:, T + t:T + t + 1]).then_inc(s_sq2, 1)
                act.wait_ge(s_v2, t + 1)
                act.activation(rstd[:, T + t:T + t + 1], ssq[:, T + t:T + t + 1], ACT.Sqrt).then_inc(s_st2, 1)

            for t in range(T):
                if t >= 2:
                    act.wait_ge(s_h2o[t % 2], 16 * (t // 2))
                    act.wait_ge(s_t2, 2 * (t - 1))
                norm2_of(t)
                act.wait_ge(s_h2, t + 1)
                act.dma_start(h2_dram[t * P:(t + 1) * P, :], h2row[:, t % 2, :]).then_inc(s_h2o[t % 2], 16)
                act.wait_ge(s_t2, 2 * t + 1)
                act.copy(h2t[:, 0:4, t * P:(t + 1) * P], bank[4][:, :].rearrange("p (a b) -> p a b", a=4)).then_inc(s_t2a, 1)
            for t in range(T):
                act.wait_ge(s_r, t + 1)
                act.activation(sig[:, t, :], bank[6 + t % 2][:, 0:E], ACT.Exp, scale=-1.0).then_inc(s_re, 1)
            for n in range(4):
                act.wait_ge(s_bp, 12 + n + 1)
                act.copy(g2bc[:, n // 2, :].rearrange("p (q k) -> p k q", k=KD)[:, 4 * (n % 2):4 * (n % 2) + 4, :],
                         bank[n % 2][:, :].rearrange("p (k q) -> p k q", k=4)).then_inc(s_ba, 1)
            act.dma_start(nfbc, norm_f.rearrange("(a n) -> a n", a=1).to_broadcast([P, D])).then_inc(s_nf, 16)

            def shared_out(t):
                act.wait_ge(s_shd, t + 1)
                if t >= 2:
                    act.wait_ge(s_shx, t - 1)
                act.copy(sh_out[:, t % 2, 0:512], bank[0][:, :])
                act.copy(sh_out[:, t % 2, 512:1024], bank[1][:, :]).then_inc(s_sho, 1)

            for t in range(T):
                act.wait_ge(s_shg, t + 1)
                if t >= 2:
                    act.wait_ge(s_shh, t - 1)
                act.copy(up_sb[:, t % 2, :], bank[2 + t % 2][:, F:2 * F])
                act.activation(sg[:, t % 2, :], bank[2 + t % 2][:, 0:F], ACT.Silu).then_inc(s_shs, 1)
                act.wait_ge(s_sht, t + 1)
                act.copy(h_t[:, t % 2, :], bank[4][:, 0:2 * P]).then_inc(s_she, 1)
                shared_out(t)

            def xt_half(b, p):
                act.wait_ge(s_xt, b + 1)
                act.copy(xg_t[:, p, 0:512], bank[0][:, :]).then_inc(s_xa, 1)

            def h_t_out(cb, p):
                act.wait_ge(s_ht, cb + 1)
                act.copy(h_t[:, p, :], bank[4][:, 0:2 * P]).then_inc(s_he, 1)

            def y_half(cb, p, scattered):
                act.wait_ge(s_y, cb + 1)
                at_least(act, s_yo[p], scattered)
                act.activation(yb[:, p, 0:512], bank[5][:, :], ACT.Copy, scale=gate_s[:, bass.ds(cb, 1)]).then_inc(s_ya, 1)

            act.wait_ge(s_tab, 1)
            xt_half(0, 0)

            def step(i, j):
                b, p = i * 4 + j, j % 2
                first = isinstance(b, int) and b == 0
                if not first:
                    h_t_out(b - 1, 1 - p)
                act.wait_ge(s_g, b + 1)
                at_least(act, s_h, b - 1)
                act.activation(sg[:, p, :], bank[2 + p][:, 0:F], ACT.Silu).then_inc(s_sg, 1)
                xt_half(b + 1, 1 - p)
                if not first:
                    y_half(b - 1, 1 - p, i * 32 + 16 * ((j - 1) // 2))

            last_g = act.value_load(trip[0:1, 0:1], min_val=FIRST_GROUPS - 1, max_val=GROUPS - 1)
            for j in range(4):
                step(0, j)
            with act.Fori(1, GROUPS) as i:
                with act.If(i < last_g + 1):
                    for j in range(4):
                        step(i, j)
            h_t_out(last_g * 4 + 3, 1)
            y_half(last_g * 4 + 3, 1, last_g * 32 + 16)

            for t in range(T):
                act.wait_ge(s_x3, t + 1)
                act.activation(yb[:, 1, :], xs[:, t, :], ACT.Square,
                               accum_out=ssq[:, 2 * T + t:2 * T + t + 1]).then_inc(s_sq3, 1)
                act.wait_ge(s_v3, t + 1)
                act.activation(rstd[:, 2 * T + t:2 * T + t + 1], ssq[:, 2 * T + t:2 * T + t + 1], ACT.Sqrt)\
                   .then_inc(s_st3, 1)

        @block.vector
        def _(dve):
            n_chain = [0]

            def link(ins):
                n_chain[0] += 1
                ins.then_inc(s_dv, 1)
                dve.wait_ge(s_dv, n_chain[0])

            dve.wait_ge(s_cexp, 1)
            link(dve.tensor_scalar_add(cw[:], cw[:], 1.0))
            link(dve.reciprocal(cw[:], cw[:]))
            dve.tensor_tensor(silu_c[:], cv[:], cw[:], ALU.mult).then_inc(s_silu, 1)
            dve.tensor_copy(identb[:], ident)
            dve.tensor_copy(onesb[:], ones)
            dve.wait_ge(s_late, 64)
            dve.tensor_copy(upper[:], early[:, D_U:D_U + P])
            dve.tensor_copy(maskb[:].rearrange("p a b -> p (a b)"), early[:, D_ML:D_ML + 2 * P]).then_inc(s_cst, 1)
            link(dve.tensor_scalar(nsink[:], psink[:], -1.0, None, ALU.mult))

            def section(s):
                dve.wait_ge(s_modpe, 2 * s + 2)
                src = bank[s % 2][:, 0:2 * KD].rearrange("p (k c) -> p k c", c=2)
                dve.tensor_tensor(mod[:, s], src, bmod[:, s, :].unsqueeze(2).to_broadcast([P, KD, 2]), ALU.add)\
                   .then_inc(s_modv, 1)

            dve.wait_ge(s_ssq, 1)
            dve.tensor_scalar(ssq[:, 0:T], ssq[:, 0:T], 1.0 / D, EPS, ALU.mult, ALU.add).then_inc(s_var, 1)
            dve.wait_ge(s_std, 1)
            link(dve.reciprocal(rstd[:, 0:T], rstd[:, 0:T]))

            def xhat(t):
                if t >= 2:
                    dve.wait_ge(s_tr, 2 * (t - 1))
                dve.tensor_scalar(xh[:, t % 2, :], xs[:, t, :], rstd[:, t:t + 1], None, ALU.mult).then_inc(s_xh, 1)

            xhat(0)
            xhat(1)
            section(0)
            section(1)
            dve.wait_ge(s_modv, 2)
            link(dve.tensor_scalar_add(a1[:], mod[:, 1], 1.0))
            dve.tensor_tensor(a1[:], a1[:], nrm[:, 0, :].unsqueeze(2).to_broadcast([P, KD, 2]), ALU.mult)\
               .then_inc(s_modv, 1)

            def h1_half(t):
                dve.wait_ge(s_tr, 2 * t + 2)
                if t == 0:
                    dve.wait_ge(s_modv, 3)
                for k in range(4, 8):
                    cond = min(t, 1)
                    last = dve.tensor_scalar(h1t[:, k, t * P:(t + 1) * P], bank[3][:, (k - 4) * P:(k - 3) * P],
                                             a1[:, k, cond:cond + 1], mod[:, 0, k, cond:cond + 1], ALU.mult, ALU.add)
                last.then_inc(s_h1b, 1)

            def qk_out(t):
                dve.wait_ge(s_qk, 2 * t + 2)
                kt = 5 if t == 0 else t - 1
                dve.tensor_copy(q_t[:, t, 4:6, :].rearrange("p a b -> p (a b)"), bank[7][:, 0:256])
                dve.tensor_copy(k_t[:, :, kt * P:(kt + 1) * P],
                                bank[7][:, 256:512].rearrange("p (a b) -> p a b", a=2)).then_inc(s_qb, 1)

            h1_half(0)
            xhat(2)
            for t in range(T):
                if t + 1 < T:
                    h1_half(t + 1)
                if t + 3 < T:
                    xhat(t + 3)
                dve.wait_ge(s_pb, 2 * t + 1)
                if t == 2:
                    dve.wait_ge(s_qk, 2)
                    dve.wait_ge(s_nk, 32)
                if t > 2:
                    dve.wait_ge(s_rot, t - 2)
                dve.tensor_copy(qk[:, t % 2, 384:768], bank[5][:, 0:384]).then_inc(s_eb, 1)
                dve.wait_ge(s_pb, 2 * t + 2)
                dve.tensor_copy(v_sb[:, t, :], bank[5][:, FD:2 * FD])
                dve.tensor_copy(qk[:, t % 2, 768:1024], bank[5][:, 0:FD]).then_inc(s_eb, 1)
                if t >= 1:
                    qk_out(t - 1)
                    dve.wait_ge(s_ea, 2 * t + 1)
                    dve.wait_ge(s_eb, 2 * t + 2)
                    src = qk[:, t % 2, :].rearrange("p (g x d) -> p g x d", g=32, x=2)
                    o = D_ROPE + (t - 1) * 128
                    cos = early[:, o:o + 64].unsqueeze(1).to_broadcast([P, 16, 64])
                    dve.tensor_tensor(rq.rearrange("p (h d) -> p h d", h=16),
                                      qk[:, t % 2, :].rearrange("p (h d) -> p h d", h=16), cos, ALU.mult)
                    dst = rtmp.rearrange("p (g x d) -> p g x d", g=32, x=2)
                    for s in range(2):
                        for x in range(2):
                            sin = early[:, o + 64 + 32 * s + 16 * x:o + 80 + 32 * s + 16 * x]
                            last = dve.tensor_tensor(dst[:, s::2, x, :], src[:, s::2, 1 - x, :],
                                                     sin.unsqueeze(1).to_broadcast([P, 16, 16]), ALU.mult)
                    link(last)
                    dve.tensor_tensor(rq, rq, rtmp, ALU.add).then_inc(s_rot, 1)
                if t < 4:
                    section(2 + t)
            qk_out(T - 1)
            dve.wait_ge(s_qk, 2 * T + 1)
            dve.tensor_copy(k_t[:, :, 4 * P:5 * P], bank[6][:, 0:256].rearrange("p (a b) -> p a b", a=2)).then_inc(s_qb, 1)
            dve.wait_ge(s_modv, 7)
            link(dve.tensor_scalar_add(a2[:], mod[:, 4], 1.0))
            link(dve.tensor_tensor(a2[:], a2[:], nrm[:, 1, :].unsqueeze(2).to_broadcast([P, KD, 2]), ALU.mult))

            n = 0
            for cc in range(2):
                for w0, wn in ((0, P), (P, 512)):
                    dve.wait_ge(s_f, 1 + 2 * n)
                    dve.tensor_copy(y_cs[:, 1, 0:wn], bank[1][:, 0:wn]).then_inc(s_fb, 1)
                    n += 1

            units = [(t, h) for t in range(T) for h in range(NH)]

            def maxima(u):
                t, h = units[u]
                n_keys = keys_of(t)[1]
                dve.wait_ge(s_s, u + 1)
                link(dve.reduce_max(mx[:, u % 2:u % 2 + 1], bank[u % 3][:, 0:n_keys], AX))
                if h == 0 and t >= 2:
                    dve.wait_ge(s_on, 2 * (t - 1))
                dve.tensor_scalar(negm[:, t % 2, h:h + 1], mx[:, u % 2:u % 2 + 1], -SCALE, nsink[:, h:h + 1],
                                  ALU.mult, ALU.min).then_inc(s_nm, 1)

            def half_tile(n):
                t, g = divmod(n, 2)
                hs = slice(6 * g, 6 * g + 6)
                dve.wait_ge(s_nm, 6 * n + 6)
                dve.tensor_tensor(den[:, n % 2, :], negm[:, t % 2, hs], psink[:, hs], ALU.add).then_inc(s_se, 1)

            def half_tile_out(n):
                t, g = divmod(n, 2)
                hs = slice(6 * g, 6 * g + 6)
                dve.wait_ge(s_sx, n + 1)
                dve.wait_ge(s_ex, 6 * n + 6)
                link(dve.tensor_tensor(den[:, n % 2, :], den[:, n % 2, :], rsum[:, t % 2, hs], ALU.add))
                link(dve.reciprocal(den[:, n % 2, :], den[:, n % 2, :]))
                dve.wait_ge(s_pvu, 6 * n + 6)
                if n >= 2:
                    dve.wait_ge(s_mt, n - 1)
                dve.tensor_tensor(on[:, n % 2, :].rearrange("p (h d) -> p h d", h=6),
                                  bank[5 + n % 2][:, 0:384].rearrange("p (h d) -> p h d", h=6),
                                  den[:, n % 2, :].unsqueeze(2).to_broadcast([P, 6, HD]), ALU.mult).then_inc(s_on, 1)

            maxima(0)
            maxima(1)
            for u in range(len(units)):
                if u + 2 < len(units):
                    maxima(u + 2)
                if u % 2 == 0:
                    dve.wait_ge(s_pt, u + 1)
                    n_keys = keys_of(units[u][0])[1]
                    if u >= 2:
                        dve.wait_ge(s_pvu, u - 1)
                    dve.tensor_copy(prob_t[:, 0, 0:n_keys], bank[3][:, 0:n_keys]).then_inc(s_ptb, 1)
                if u % 6 == 0 and u:
                    half_tile(u // 6 - 1)
                if u % 6 == 1 and u > 6:
                    half_tile_out(u // 6 - 1)
            half_tile(9)
            half_tile_out(9)

            def diagonals(n, col):
                if n >= 2:
                    dve.wait_ge(s_bp, n - 1)
                dve.tensor_tensor(dg[:, n % 2], ident.unsqueeze(1).to_broadcast([P, 4, P]),
                                  col.unsqueeze(2).to_broadcast([P, 4, P]), ALU.mult).then_inc(s_dg, 1)

            dve.wait_ge(s_ex, len(units))
            for v in range(6):
                col = (mod[:, 2], a2[:], mod[:, 3])[v // 2]
                for hf in range(2):
                    diagonals(2 * v + hf, col[:, 4 * hf:4 * hf + 4, v % 2])

            def h2t_half(t):
                dve.wait_ge(s_t2, 2 * t + 2)
                dve.tensor_copy(h2t[:, 4:8, t * P:(t + 1) * P], bank[5][:, :].rearrange("p (a b) -> p a b", a=4))\
                   .then_inc(s_t2b, 1)

            dve.wait_ge(s_ba, 12)
            for t in range(T):
                cond = min(t, 1)
                for hf in range(2):
                    dve.wait_ge(s_op, 2 * t + hf + 1)
                    cols = slice(512 * hf, 512 * hf + 512)
                    dve.tensor_tensor(x2_tmp[:, cols], bank[2 * (t % 2) + hf][:, :], bc[:, cond, cols], ALU.mult)\
                       .then_inc(s_x2, 1)
                dve.wait_ge(s_x2, 2 * t + 2)
                dve.tensor_tensor(xs[:, t, :], xs[:, t, :], x2_tmp, ALU.add).then_inc(s_x2r, 1)
                dve.wait_ge(s_sq2, t + 1)
                r = slice(T + t, T + t + 1)
                dve.tensor_scalar(ssq[:, r], ssq[:, r], 1.0 / D, EPS, ALU.mult, ALU.add).then_inc(s_v2, 1)
                dve.wait_ge(s_st2, t + 1)
                link(dve.reciprocal(rstd[:, r], rstd[:, r]))
                link(dve.scalar_tensor_tensor(h2row[:, t % 2, :], xs[:, t, :], rstd[:, r], bc[:, 2 + cond, :],
                                              ALU.mult, ALU.mult))
                dve.tensor_tensor(h2row[:, t % 2, :], h2row[:, t % 2, :], bc[:, 4 + cond, :], ALU.add).then_inc(s_h2, 1)
                h2t_half(t)

            for n in range(4):
                if n:
                    dve.wait_ge(s_bp, 12 + n)
                col = mod[:, 5, 4 * (n % 2):4 * (n % 2) + 4, n // 2]
                dve.tensor_tensor(dg2, ident.unsqueeze(1).to_broadcast([P, 4, P]),
                                  col.unsqueeze(2).to_broadcast([P, 4, P]), ALU.mult).then_inc(s_dg, 1)

            dve.wait_ge(s_late2, 32)
            for t in range(T):
                sg_t = sig[:, t, :]
                dve.wait_ge(s_re, t + 1)
                link(dve.tensor_scalar_add(sg_t, sg_t, 1.0))
                link(dve.reciprocal(sg_t, sg_t))
                link(dve.tensor_tensor(sc[:], sg_t, rbias[:], ALU.add))
                for g in range(8):
                    last = dve.max(g8[:, g, :], sc[:, 8 * g:8 * g + 8])
                link(last)
                link(dve.tensor_tensor(gsc[:], g8[:, :, 0], g8[:, :, 1], ALU.add))
                link(dve.max(top[:], gsc[:]))
                link(dve.max_index(topi[:], top[:], gsc[:]))
                link(dve.tensor_copy(gif[:], topi[:]))
                link(dve.tensor_tensor(geq[:], iota[:, 0:8].unsqueeze(2).to_broadcast([P, 8, 4]),
                                       gif[:, 0:4].unsqueeze(1).to_broadcast([P, 8, 4]), ALU.is_equal))
                link(dve.tensor_reduce(gpen[:], geq[:], AX, ALU.add))
                link(dve.tensor_scalar(gpen[:], gpen[:], -1.0, -NEG, ALU.add, ALU.mult))
                link(dve.tensor_tensor(sc[:].rearrange("p (g e) -> p g e", g=8), sc[:].rearrange("p (g e) -> p g e", g=8),
                                       gpen[:].unsqueeze(2).to_broadcast([P, 8, 8]), ALU.add))
                link(dve.max(top[:], sc[:]))
                link(dve.max_index(topi[:], top[:], sc[:]))
                link(dve.tensor_copy(eif[:, t, :], topi[:]))
                link(dve.tensor_tensor(eq_ke, iota[:, 0:E].unsqueeze(1).to_broadcast([P, TOPK, E]),
                                       eif[:, t, :].unsqueeze(2).to_broadcast([P, TOPK, E]), ALU.is_equal))
                with nc.allow_low_precision("zeros and ones are exact"):
                    dve.tensor_reduce(maskm[:, t, :], eq_ke.rearrange("p k e -> p e k"), AX, ALU.add).then_inc(s_mm, 1)
                link(dve.tensor_tensor(eq_tmp, eq_ke, sg_t.unsqueeze(1).to_broadcast([P, TOPK, E]), ALU.mult))
                link(dve.tensor_reduce(gate[:, t, :], eq_tmp, AX, ALU.add))
                link(dve.tensor_reduce(gsum[:, 0:1], gate[:, t, :], AX, ALU.add))
                link(dve.reciprocal(gsum[:, 1:2], gsum[:, 0:1]))
                dve.tensor_scalar(gate[:, t, :], gate[:, t, :], gsum[:, 1:2], ROUTED, ALU.mult, ALU.mult).then_inc(s_rs, 1)

            dve.wait_ge(s_pos, 1)
            dve.wait_ge(s_rs, T)
            pos, cnt = bank[6][:, 0:T * E], bank[7][:, 0:E]
            blk2, jm2 = blk[:].rearrange("p t e -> p (t e)"), jmap[:].rearrange("p t e -> p (t e)")
            posf = a_oh.rearrange("p k q -> p (k q)")[:, 0:T * E]
            link(dve.tensor_scalar(xb[:], cnt, float(P), None, ALU.is_gt))
            link(dve.tensor_scalar(blk2, pos, float(P), None, ALU.is_ge))
            for m in range(2, T):
                link(dve.scalar_tensor_tensor(xb[:], cnt, float(m * P), xb[:], ALU.is_gt, ALU.add))
                link(dve.scalar_tensor_tensor(blk2, pos, float(m * P), blk2, ALU.is_ge, ALU.add))
            link(dve.tensor_tensor_scan(xinc[:], ones[:, 0:E], xb[:], 0.0, ALU.mult, ALU.add))
            link(dve.tensor_tensor(xb[:], xinc[:], xb[:], ALU.subtract))
            link(dve.scalar_tensor_tensor(xb[:], xb[:], float(E - 1), iota[:, 0:E], ALU.add, ALU.subtract))
            link(dve.tensor_tensor(jmap[:], blk[:], xb[:].unsqueeze(1).to_broadcast([P, T, E]), ALU.add))
            link(dve.scalar_tensor_tensor(jm2, blk2, 0.0, jm2, ALU.is_gt, ALU.mult))
            link(dve.tensor_tensor(jmap[:], jmap[:], iota[:, 0:E].unsqueeze(1).to_broadcast([P, T, E]), ALU.add))
            link(dve.tensor_scalar(blk2, blk2, -float(P), None, ALU.mult))
            link(dve.tensor_tensor(blk2, blk2, pos, ALU.add))
            link(dve.tensor_scalar(tripf[:], iota[0:1, 0:16], 4.0, xinc[0:1, E - 1:E], ALU.mult, ALU.is_lt))
            link(dve.tensor_reduce(tripn[:], tripf[:], AX, ALU.add))
            link(dve.tensor_scalar(tripn[:], tripn[:], float(FIRST_GROUPS - 1), None, ALU.add))
            link(dve.tensor_copy(trip[:], tripn[:]))
            link(dve.tensor_copy(eidf[:], iota[0:1, 0:NT]))
            for q0 in range(0, XBLK, 8):
                cmp = eq_tmp[0:1]
                link(dve.tensor_tensor(cmp, xinc[0:1, :].unsqueeze(1).to_broadcast([1, 8, E]),
                                       iota[0:1, q0:q0 + 8].unsqueeze(2).to_broadcast([1, 8, E]), ALU.is_le))
                link(dve.tensor_reduce(eidf[0:1, E + q0:E + q0 + 8], cmp, AX, ALU.add))
            link(dve.tensor_scalar(eidf[:], eidf[:], float(E - 1), None, ALU.min))
            link(dve.tensor_copy(eid[:], eidf[:]))
            dve.wait_ge(s_h2o[0], 48)
            dve.wait_ge(s_h2o[1], 32)
            for t in range(T):
                link(dve.tensor_tensor(eq_ke, iota[:, 0:E].unsqueeze(1).to_broadcast([P, TOPK, E]),
                                       eif[:, t, :].unsqueeze(2).to_broadcast([P, TOPK, E]), ALU.is_equal))
                for m, src in enumerate((blk, jmap)):
                    link(dve.tensor_tensor(eq_tmp, eq_ke, src[:, t, :].unsqueeze(1).to_broadcast([P, TOPK, E]), ALU.mult))
                    link(dve.tensor_reduce(pk[:, m, :], eq_tmp, AX, ALU.add))
                link(dve.tensor_scalar(vk[:], iota[:, 0:TOPK], keep[:, C_VT + t:C_VT + t + 1], None, ALU.add))
                if t:
                    dve.wait_ge(s_tb, t)
                dve.tensor_tensor(a_oh, iota.unsqueeze(1).to_broadcast([P, TOPK, P]),
                                  pk[:, 0, :].unsqueeze(2).to_broadcast([P, TOPK, P]), ALU.is_equal)
                link(dve.tensor_tensor(b_oh[:, :, 1, :], iota[:, 0:NT].unsqueeze(1).to_broadcast([P, TOPK, NT]),
                                       pk[:, 1, :].unsqueeze(2).to_broadcast([P, TOPK, NT]), ALU.is_equal))
                link(dve.tensor_tensor(b_oh[:, :, 0, :], b_oh[:, :, 1, :],
                                       vk[:].unsqueeze(2).to_broadcast([P, TOPK, NT]), ALU.mult))
                dve.tensor_tensor(b_oh[:, :, 1, :], b_oh[:, :, 1, :],
                                  gate[:, t, :].unsqueeze(2).to_broadcast([P, TOPK, NT]), ALU.mult).then_inc(s_oh, 1)
            dve.wait_ge(s_tb, T)
            link(dve.tensor_scalar(row_i[:], bank[6][:, 0:NT], float(NROW), None, ALU.add))
            link(dve.tensor_copy(gate_s[:], bank[6][:, NT:2 * NT]))
            dve.tensor_single_scalar(tok_i[:], row_i[:], 3, ALU.logical_shift_right).then_inc(s_tab, 1)

            dve.wait_ge(s_tab, 1)

            def xt_half(b, p):
                dve.wait_ge(s_xt, b + 1)
                dve.tensor_copy(xg_t[:, p, 512:1024], bank[1][:, :]).then_inc(s_xb, 1)

            def y_half(cb, p, scattered):
                dve.wait_ge(s_y, cb + 1)
                at_least(dve, s_yo[p], scattered)
                dve.tensor_scalar(yb[:, p, 512:1024], bank[6][:, :], gate_s[:, bass.ds(cb, 1)], None, ALU.mult)\
                   .then_inc(s_yb, 1)

            xt_half(0, 0)

            def step(i, j):
                b, p = i * 4 + j, j % 2
                dve.wait_ge(s_sg, b + 1)
                at_least(dve, s_ht, b - 1)
                dve.tensor_tensor(hh[:, p, :], sg[:, p, :], bank[2 + p][:, F:2 * F], ALU.mult).then_inc(s_h, 1)
                xt_half(b + 1, 1 - p)
                if not (isinstance(b, int) and b == 0):
                    y_half(b - 1, 1 - p, i * 32 + 16 * ((j - 1) // 2))

            last_g = dve.value_load(trip[0:1, 0:1], min_val=FIRST_GROUPS - 1, max_val=GROUPS - 1)
            for j in range(4):
                step(0, j)
            with dve.Fori(1, GROUPS) as i:
                with dve.If(i < last_g + 1):
                    for j in range(4):
                        step(i, j)
            y_half(last_g * 4 + 3, 1, last_g * 32 + 16)

            dve.wait_ge(s_nf, 16)
            dve.wait_ge(s_shx, T)
            for t in range(T):
                cond = min(t, 1)
                rows = ring[:, (t % 3) * 8192:(t % 3 + 1) * 8192]
                dve.wait_ge(s_row[t % 3], 16 * (t // 3 + 1))
                link(dve.tensor_tensor(rows[:, 0:4096], rows[:, 0:4096], rows[:, 4096:8192], ALU.add))
                link(dve.tensor_tensor(rows[:, 0:2048], rows[:, 0:2048], rows[:, 2048:4096], ALU.add))
                link(dve.tensor_tensor(rows[:, 0:1024], rows[:, 0:1024], rows[:, 1024:2048], ALU.add))
                dve.tensor_tensor(yb[:, 0, :], rows[:, 0:1024], g2bc[:, cond, :], ALU.mult).then_inc(s_fr, 1)
                dve.wait_ge(s_fr, t + 1)
                dve.tensor_tensor(xs[:, t, :], xs[:, t, :], yb[:, 0, :], ALU.add).then_inc(s_x3, 1)
                r = slice(2 * T + t, 2 * T + t + 1)
                dve.wait_ge(s_sq3, t + 1)
                dve.tensor_scalar(ssq[:, r], ssq[:, r], 1.0 / D, EPS, ALU.mult, ALU.add).then_inc(s_v3, 1)
                dve.wait_ge(s_st3, t + 1)
                link(dve.reciprocal(rstd[:, r], rstd[:, r]))
                dve.scalar_tensor_tensor(xs[:, t, :], xs[:, t, :], rstd[:, r], nfbc, ALU.mult, ALU.mult).then_inc(s_fin, 1)

        @block.tensor
        def _(pe):
            def mod_chunk(n):
                s, kh = divmod(n, 2)
                arrived(pe, "mod", n)
                w = view(ring, slot(where["mod", n]), 4, D).rearrange("p k (q o) -> p k o q", o=KD)
                for o in range(KD):
                    for k in range(4):
                        last = pe.matmul(bank[s % 2][:, 2 * o:2 * o + 2], w[:, k, o, :], silu_c[:, :, 4 * kh + k],
                                         start=(kh == 0 and o == 0 and k == 0), stop=(kh == 1 and k == 3),
                                         skip_group_check=True)
                last.then_inc(s_modpe, 1)

            def xhat_t(t):
                pe.wait_ge(s_xh, t + 1)
                v = xh[:, t % 2, :].rearrange("p (q k) -> p k q", k=KD)
                for hf in range(2):
                    if t:
                        pe.wait_ge((s_h1a, s_h1b)[hf], t)
                    for k in range(4):
                        last = pe.transpose(bank[2 + hf][:, k * P:(k + 1) * P], v[:, 4 * hf + k, :], ident)
                    last.then_inc(s_tr, 1)

            def projection(t, groups):
                pe.wait_ge(s_h1a, t + 1)
                pe.wait_ge(s_h1b, t + 1)
                for g in groups:
                    if t or g >= 2:
                        pe.wait_ge((s_ea, s_eb)[g % 2], 2 * t + g // 2)
                    n = (384, 384, FD, 2 * FD)[g]
                    for k in range(KD):
                        w = view(ring, slot(where["win", k // 4]), 4, PROJ)[:, k % 4, :]
                        if g < 2:
                            rhs = w[:, FD + 384 * g:FD + 384 * (g + 1)].rearrange("p (b g d) -> p g b d", b=2, g=3)
                        else:
                            rhs = w[:, 0:FD] if g == 2 else w[:, FD + NH * HD:PROJ]
                        last = pe.matmul(bank[4 + g % 2][:, 0:n], h1t[:, k, t * P:(t + 1) * P], rhs,
                                         start=(k == 0), stop=(k == KD - 1))
                    last.then_inc((s_pa, s_pb)[g % 2], 1)

            def qk_t(t):
                if t:
                    pe.wait_ge(s_rot, t)
                    src = rq
                    pe.wait_ge(s_qa, t)
                    pe.wait_ge(s_qb, t)
                else:
                    pe.wait_ge(s_ea, 1)
                    pe.wait_ge(s_eb, 2)
                    src = qk[:, 0, :]
                for n in range(8):
                    last = pe.transpose(bank[6 + n // 4][:, (n % 4) * P:(n % 4 + 1) * P], src[:, n * P:(n + 1) * P], ident)
                    if n % 4 == 3:
                        last.then_inc(s_qk, 1)

            pe.wait_ge(s_silu, 1)
            pe.wait_ge(s_small, 96)
            mod_chunk(0)
            xhat_t(0)
            mod_chunk(1)
            mod_chunk(2)
            mod_chunk(3)
            for t in range(T):
                if t + 1 < T:
                    xhat_t(t + 1)
                if t == 0:
                    arrived(pe, "win", 0)
                    arrived(pe, "win", 1)
                projection(t, (0, 1))
                if t < 4:
                    pe.wait_ge(s_modv, t + 1 if t < 2 else t + 2)
                    mod_chunk(4 + 2 * t)
                projection(t, (2, 3))
                if t < 4:
                    mod_chunk(5 + 2 * t)
                if t:
                    qk_t(t - 1)
            qk_t(T - 1)
            pe.wait_ge(s_qa, T)
            pe.wait_ge(s_late, 64)
            pe.wait_ge(s_wf, 64)
            for a in range(2):
                last = pe.transpose(bank[6][:, a * P:(a + 1) * P], kctx[:, a * P:(a + 1) * P], ident)
            last.then_inc(s_qk, 1)

            pe.wait_ge(s_modv, 7)
            for x, o in ((0, D_C64), (1, D_S64)):
                for cc in range(2):
                    last = pe.matmul(bank[0][:, (2 * x + cc) * P:(2 * x + cc + 1) * P], early[:, o:o + P], w_bd[:, cc, :],
                                     start=True, stop=True)
            last.then_inc(s_m, 1)
            pe.wait_ge(s_me, 1)
            pe.wait_ge(s_ea, 2 * T)
            pe.wait_ge(s_eb, 2 * T)
            arrived(pe, "dft", 0)
            dft = view(ring, slot(where["dft", 0]), LAT, 2, 512)
            n = 0
            for cc in range(2):
                for w0, wn in ((0, P), (P, 512)):
                    for x in range(2):
                        if w0 == 0:
                            o = D_DFT + x * P
                            last = pe.matmul(bank[x][:, 0:P], u_sb[:, 0, cc * P:(cc + 1) * P], early[:, o:o + P],
                                             start=True, stop=True)
                        else:
                            for k in range(LAT):
                                last = pe.matmul(bank[x][:, :], u_sb[:, 1 + k, cc * P:(cc + 1) * P], dft[:, k, x, :],
                                                 start=(k == 0), stop=(k == LAT - 1))
                    last.then_inc(s_f, 1)
                    pe.wait_ge(s_fa, 2 * n + 1)
                    pe.wait_ge(s_fb, n + 1)
                    for x in range(2):
                        last = pe.matmul(bank[2][:, 0:wn], m_cs[:, x, cc, :], y_cs[:, x, 0:wn], start=(x == 0), stop=(x == 1))
                    last.then_inc(s_f, 1)
                    n += 1

            pe.wait_ge(s_fa, 8)
            pe.wait_ge(s_qa, T)
            pe.wait_ge(s_qb, T + 1)
            pe.wait_ge(s_cst, 1)
            units = [(t, h) for t in range(T) for h in range(NH)]

            def scores(u):
                t, h = units[u]
                tiles, n_keys = keys_of(t)
                a, b, g = h // 6, (h % 6) // 3, h % 3
                if u >= 3:
                    pe.wait_ge(s_ex, u - 2)
                q = q_t[64 * b:64 * b + 64, t, 3 * a + g, :]
                out = bank[u % 3]
                if t == 0:
                    pe.matmul(out[:, 0:P], q, k_t[64 * b:64 * b + 64, a, 5 * P:6 * P], start=True, stop=True)\
                      .then_inc(s_s, 1)
                    return
                lo, n_win = tiles[0], len(tiles) - 1
                left, right = lo == t - 2, tiles[n_win - 1] == t
                pe.matmul(out[:, 0:n_win * P], q, k_t[64 * b:64 * b + 64, a, lo * P:(lo + n_win) * P],
                          start=True, stop=False)
                if left:
                    pe.matmul(out[:, 0:P], identb[:], maskb[:, 0, :], start=False, stop=not right)
                if right:
                    pe.matmul(out[:, (n_win - 1) * P:n_win * P], identb[:], maskb[:, 1, :], start=False, stop=True)
                pe.matmul(out[:, n_win * P:n_keys], q, k_t[64 * b:64 * b + 64, a, 4 * P:5 * P], start=True, stop=True)\
                  .then_inc(s_s, 1)

            def probs_t(u):
                tiles, n_keys = keys_of(units[u][0])
                pe.wait_ge(s_ex, u + 1)
                if u >= 2:
                    pe.wait_ge((s_ptb, s_pta)[u % 2], u // 2)
                for m in range(len(tiles)):
                    last = pe.transpose(bank[3 + u % 2][:, m * P:(m + 1) * P], prob[:, u % 2, m * P:(m + 1) * P], ident)
                last.then_inc(s_pt, 1)

            def values(u):
                t, h = units[u]
                tiles, n_keys = keys_of(t)
                n, kv = u // 6, h // 3
                if u % 6 == 0 and n >= 2:
                    pe.wait_ge(s_on, n - 1)
                pe.wait_ge((s_ptb, s_pta)[u % 2], u // 2 + 1)
                for m, kt in enumerate(tiles):
                    vt = {5: 0, 4: T}.get(kt, kt + 1)
                    last = pe.matmul(bank[5 + n % 2][:, (u % 6) * HD:(u % 6 + 1) * HD], prob_t[:, u % 2, m * P:(m + 1) * P],
                                     v_sb[:, vt, kv * HD:(kv + 1) * HD], start=(m == 0), stop=(m == len(tiles) - 1))
                last.then_inc(s_pvu, 1)

            def mix(n):
                pe.wait_ge(s_on, n + 1)
                if n:
                    pe.wait_ge(s_mta, n)
                for m in range(3):
                    last = pe.transpose(bank[7][:, m * P:(m + 1) * P], on[:, n % 2, m * P:(m + 1) * P], ident)
                last.then_inc(s_mt, 1)

            scores(0)
            scores(1)
            for u in range(len(units)):
                if u + 2 < len(units):
                    scores(u + 2)
                probs_t(u)
                if u:
                    values(u - 1)
                if u % 6 == 3 and u > 6:
                    mix(u // 6 - 1)
            values(len(units) - 1)
            mix(9)

            def spread(n, src):
                pe.wait_ge(s_dg, n + 1)
                if n >= 2:
                    pe.wait_ge(s_ba, n - 1)
                pe.matmul(bank[n % 2][:, :], ones, src.rearrange("p a b -> p (a b)"), start=True, stop=True).then_inc(s_bp, 1)

            for n in range(12):
                spread(n, dg[:, n % 2])

            def out_projection(t):
                if t >= 2:
                    pe.wait_ge(s_x2, 2 * (t - 1))
                for hf in range(2):
                    for k in range(KD):
                        w = view(ring, slot(where["wout", k // 4]), 4, D)[:, k % 4, 512 * hf:512 * hf + 512]
                        last = pe.matmul(bank[2 * (t % 2) + hf][:, :], mix_t[:, k, t * P:(t + 1) * P], w,
                                         start=(k == 0), stop=(k == KD - 1))
                    last.then_inc(s_op, 1)

            def h2_t(t):
                pe.wait_ge(s_h2, t + 1)
                if t:
                    pe.wait_ge(s_t2a, t)
                    pe.wait_ge(s_t2b, t)
                v = h2row[:, t % 2, :].rearrange("p (q k) -> p k q", k=KD)
                for k in range(KD):
                    last = pe.transpose(bank[4 + k // 4][:, (k % 4) * P:(k % 4 + 1) * P], v[:, k, :], ident)
                    if k % 4 == 3:
                        last.then_inc(s_t2, 1)

            def router(t):
                pe.wait_ge(s_t2a, t + 1)
                pe.wait_ge(s_t2b, t + 1)
                if t >= 2:
                    pe.wait_ge(s_re, t - 1)
                for k in range(KD):
                    last = pe.matmul(bank[6 + t % 2][:, 0:E], h2t[:, k, t * P:(t + 1) * P], wr[:, k, :],
                                     start=(k == 0), stop=(k == KD - 1))
                last.then_inc(s_r, 1)

            arrived(pe, "wout", 0)
            arrived(pe, "wout", 1)
            pe.wait_ge(s_mta, 10)
            pe.wait_ge(s_ba, 12)
            pe.wait_ge(s_late2, 32)
            out_projection(0)
            for t in range(T):
                if t + 1 < T:
                    out_projection(t + 1)
                h2_t(t)
            for t in range(T):
                router(t)
            pe.wait_ge(s_x2, 2 * T)
            for n in range(4):
                spread(12 + n, dg2)

            def gate_up(s, out, x_of, ks):
                w = w_gu(s)
                for k in ks:
                    last = pe.matmul(bank[out][:, :], x_of(k), w[:, k], start=(k == 0), stop=(k == KD - 1))
                return last

            def h_transposes(src):
                v = src.rearrange("p (q j) -> p j q", j=2)
                for j in range(2):
                    last = pe.transpose(bank[4][:, j * P:(j + 1) * P], v[:, j, :], ident)
                return last

            def down(s, outs, src):
                w = w_dn(s)
                for hf in range(2):
                    for j in range(2):
                        last = pe.matmul(bank[outs[hf]][:, :], src[:, j * P:(j + 1) * P], w[:, j, 512 * hf:512 * hf + 512],
                                         start=(j == 0), stop=(j == 1))
                return last

            def shared_down(t):
                pe.wait_ge(s_shh, t + 1)
                if t:
                    pe.wait_ge(s_she, t)
                h_transposes(hh[:, t % 2, :]).then_inc(s_sht, 1)
                pe.wait_ge(s_she, t + 1)
                if t:
                    pe.wait_ge(s_sho, t)
                down(item_slot(0), (0, 1), h_t[:, t % 2, :]).then_inc(s_shd, 1)

            pe.wait_ge(s_ring[item_slot(0)], experts_in(0, item_slot(0)))
            pe.wait_ge(s_ba, 16)
            for t in range(T):
                if t >= 2:
                    pe.wait_ge(s_shs, t - 1)
                gate_up(item_slot(0), 2 + t % 2, lambda k: h2t[:, k, t * P:(t + 1) * P], range(KD)).then_inc(s_shg, 1)
                if t:
                    shared_down(t - 1)
            pe.wait_ge(s_mm, T)
            pe.wait_ge(s_re, T)
            for t in range(T):
                for o in range(t + 1):
                    pe.matmul(bank[6][:, t * E:(t + 1) * E], upper[:] if o == t else onesb[:], maskm[:, o, :],
                              start=(o == 0), stop=(o == t))
            for o in range(T):
                last = pe.matmul(bank[7][:, 0:E], onesb[:], maskm[:, o, :], start=(o == 0), stop=(o == T - 1))
            last.then_inc(s_pos, 1)
            shared_down(T - 1)
            for t in range(T):
                pe.wait_ge(s_oh, t + 1)
                for k in range(TOPK):
                    last = pe.matmul(bank[6][:, 0:2 * NT], a_oh[:, k, :], b_oh[:, k].rearrange("p a b -> p (a b)"),
                                     start=(t == 0 and k == 0), stop=(t == T - 1 and k == TOPK - 1))
                last.then_inc(s_tb, 1)

            def block_transposes(b, p, gathered):
                pe.wait_ge(s_xg[p], gathered)
                v = xg[:, p, :].rearrange("p (q k) -> p k q", k=KD)
                for k in range(KD):
                    last = pe.transpose(bank[k // 4][:, (k % 4) * P:(k % 4 + 1) * P], v[:, k, :], ident)
                last.then_inc(s_xt, 1)

            def block_h(cb, p):
                pe.wait_ge(s_h, cb + 1)
                at_least(pe, s_he, cb)
                h_transposes(hh[:, p, :]).then_inc(s_ht, 1)

            def block_down(cb, p, s):
                pe.wait_ge(s_he, cb + 1)
                at_least(pe, s_ya, cb)
                at_least(pe, s_yb, cb)
                down(s, (5, 6), h_t[:, p, :]).then_inc(s_y, 1)

            pe.wait_ge(s_tab, 1)
            pe.wait_ge(s_sho, T)
            block_transposes(0, 0, 16)

            def step(i, j):
                b, p, s = i * 4 + j, j % 2, item_slot(j + 1)
                first = isinstance(b, int) and b == 0
                pe.wait_ge(s_ring[s], 16 * uses[s] + (i + (1 if j < 3 else 2)) * 48)
                pe.wait_ge(s_xa, b + 1)
                pe.wait_ge(s_xb, b + 1)
                at_least(pe, s_h, b - 1)
                gate_up(s, 2 + p, lambda k: xg_t[:, p, k * P:(k + 1) * P], range(0, 4))
                if not first:
                    block_h(b - 1, 1 - p)
                gate_up(s, 2 + p, lambda k: xg_t[:, p, k * P:(k + 1) * P], range(4, 8)).then_inc(s_g, 1)
                block_transposes(b + 1, 1 - p, (i * 2 + (j + 1) // 2 + 1) * 16)
                if not first:
                    block_down(b - 1, 1 - p, item_slot(j))

            last_g = pe.value_load(trip[0:1, 0:1], min_val=FIRST_GROUPS - 1, max_val=GROUPS - 1)
            for j in range(4):
                step(0, j)
            with pe.Fori(1, GROUPS) as i:
                with pe.If(i < last_g + 1):
                    for j in range(4):
                        step(i, j)
            block_h(last_g * 4 + 3, 1)
            block_down(last_g * 4 + 3, 1, item_slot(4))


_INS = ["x_prompt", "x_sample", "cache_k", "cache_v", "c", "c_ctx", "w_mod", "b_mod", "norm1", "w_in", "w_fourier",
        "sink", "w_out", "norm2", "w_router", "router_bias", "w_gate", "w_up", "w_down", "ws_gate", "ws_up",
        "ws_down", "norm_f"]
_OUTS = [("y_prompt", (1, P, D)), ("y_sample", (1, LAT * P, D)), ("new_k", (1, 1, P, NKV, HD)),
         ("new_v", (1, 1, P, NKV, HD))]


def kernel(**inputs):
    import concourse.bacc as bacc
    from concourse.bass_utils import run_bass_kernel_spmd

    nc = bacc.Bacc("TRN2", target_bir_lowering=False, num_devices=1)
    arrays, args = {}, []
    given = [(n, np.ascontiguousarray(inputs[n])) for n in _INS]
    given += list(zip(("keep_c", "early_c", "dft_c"), shape_constants()))
    for name, a in given:
        arrays[f"in_{name}"] = a
        args.append(nc.dram_tensor(f"in_{name}", a.shape, mybir.dt.from_np(a.dtype), kind="ExternalInput").ap())
    for name, shape in _OUTS:
        args.append(nc.dram_tensor(f"out_{name}", shape, F32, kind="ExternalOutput").ap())
    build(nc, *args)
    r = run_bass_kernel_spmd(nc, [arrays], core_ids=[0])
    return tuple(r.results[0][f"out_{name}"] for name, _ in _OUTS)
```

```python
from contextlib import ExitStack

import numpy as np
import concourse.bass as bass
from concourse import mybir

F32 = mybir.dt.float32
BF16 = mybir.dt.bfloat16
I32 = mybir.dt.int32
U32 = mybir.dt.uint32
ALU = mybir.AluOpType
ACT = mybir.ActivationFunctionType
AX = mybir.AxisListType.X

P = 128
D = 1024
KD = D // P
LAT = 4
T = 1 + LAT
NTOK = T * P
HD = 64
NH = 12
NKV = 4
FD = 256
PROJ = 1536
E = 64
TOPK = 8
F = 256
EPS = 1e-6
SCALE = HD ** -0.5
NEG = -1e30
ROUTED = 2.5
BLOCKS_MAX = E + (NTOK * TOPK) // (P + 1)
GROUPS = -(-BLOCKS_MAX // 4)
XBLK = 4 * GROUPS - E
NT = 4 * GROUPS + 2
NROW = NTOK * TOPK
SLOT = 6144
PIECES = 6 * KD // 2

C_ID, C_ONE, C_IOTA, C_VT, C_N = 0, 128, 256, 384, 392
D_ROPE, D_DFT, D_C64, D_S64, D_U, D_ML, D_MR, D_N = 0, 512, 768, 896, 1024, 1152, 1280, 1408


def shape_constants():
    a = np.arange(P)
    keep = np.zeros((P, C_N), np.float32)
    keep[:, C_ID:C_ID + P] = np.eye(P)
    keep[:, C_ONE:C_ONE + P] = 1.0
    keep[:, C_IOTA:C_IOTA + P] = a[None, :]
    for t in range(T):
        keep[:, C_VT + t] = (t * P + a) * TOPK - NROW
    early = np.zeros((P, D_N), np.float64)
    inv = (10000.0 ** (-np.arange(16) / 16.0)).astype(np.float32)
    pos = np.arange(LAT * P)
    for half, where in ((0, pos // 64), (1, pos % 64)):
        ang = (where.astype(np.float32)[:, None] * inv[None, :]).astype(np.float32).astype(np.float64)
        c, s = np.cos(ang), np.sin(ang)
        for t in range(LAT):
            r = slice(t * P, (t + 1) * P)
            o = D_ROPE + t * 128 + half * 32
            early[:, o:o + 16], early[:, o + 16:o + 32] = c[r], c[r]
            early[:, o + 64:o + 80], early[:, o + 80:o + 96] = -s[r], s[r]
    w = 2 * np.pi * np.outer(a, a) / P
    early[:, D_DFT:D_DFT + 128] = np.cos(w) / P ** 0.5
    early[:, D_DFT + 128:D_DFT + 256] = np.sin(w) / P ** 0.5
    m = np.arange(HD)
    w = 2 * np.pi * np.outer(m, m) / HD
    for o, v in ((D_C64, np.cos(w) / 8), (D_S64, -np.sin(w) / 8)):
        early[0:64, o:o + 64] = v
        early[64:128, o + 64:o + 128] = v
    early[:, D_U:D_U + P] = a[:, None] < a[None, :]
    early[:, D_ML:D_ML + P] = np.where(a[None, :] >= a[:, None], 0.0, NEG)
    early[:, D_MR:D_MR + P] = np.where(a[None, :] <= a[:, None], 0.0, NEG)
    n = LAT * P
    w = 2 * np.pi * (np.outer(np.arange(n), np.arange(n)) % n) / n
    dft = np.stack([np.cos(w), np.sin(w)], 1) / n ** 0.5
    dft = dft.reshape(LAT, P, 2, n).transpose(1, 0, 2, 3).reshape(P, LAT * 2 * n)
    return keep, early.astype(np.float32), np.ascontiguousarray(dft.astype(np.float32))


def build(nc, x_prompt, x_sample, cache_k, cache_v, c, c_ctx, w_mod, b_mod, norm1, w_in, w_fourier, sink,
          w_out, norm2, w_router, router_bias, w_gate, w_up, w_down, ws_gate, ws_up, ws_down, norm_f,
          keep_c, early_c, dft_c, y_prompt, y_sample, new_k, new_v):
    ctx = ExitStack()
    with ctx:
        def sb(name, shape, dt=F32):
            return ctx.enter_context(nc.sbuf_tensor(name, shape, dt))

        def sem(name):
            return ctx.enter_context(nc.semaphore(name))

        h2_dram = nc.dram_tensor("h2_rows", (NTOK, D), F32, kind="Internal").ap()
        y_dram = nc.dram_tensor("expert_rows", (NROW, D), F32, kind="Internal").ap()

        ring = sb("ring", [P, 4 * SLOT])
        xs = sb("xs", [P, T, D])
        reg_h = sb("reg_h", [P, 5120])
        reg_p = sb("reg_p", [P, 7680])
        reg_b = sb("reg_b", [P, 6144])
        reg_y = sb("reg_y", [P, 2560])

        def view(reg, off, *dims):
            n = int(np.prod(dims))
            v = reg[:, off:off + n]
            if len(dims) == 2:
                v = v.rearrange("p (a b) -> p a b", a=dims[0])
            if len(dims) == 3:
                v = v.rearrange("p (a b c) -> p a b c", a=dims[0], b=dims[1])
            return v

        def slot(s):
            return s * SLOT

        def keys_of(t):
            if t == 0:
                return [5], P
            tiles = list(range(max(0, t - 2), min(LAT - 1, t) + 1)) + [4]
            return tiles, P * len(tiles)

        turn = (2, 3, 1, 4, 0)

        s3 = slot(3)
        xh = view(ring, s3, 2, D)
        prob = view(ring, s3 + 2048, 2, 512)
        prob_t = view(ring, s3 + 3072, 2, 512)
        qk = view(ring, s3 + 4096, 2, D)
        h1t = view(reg_h, 0, KD, NTOK)
        mix_t = view(reg_h, 0, KD, NTOK)
        u_sb = view(reg_p, 0, T, FD)
        v_sb = view(reg_p, 1280, T + 1, FD)
        q_t = view(reg_p, 2816, T, 6, P)
        on = view(reg_p, 6656, 2, 384)
        k_t = view(reg_b, 0, 2, 6 * P)
        y_cs = view(reg_b, 1536, 2, 512)
        rq = view(reg_b, 2560, D)
        rtmp = view(reg_b, 3584, D)
        kctx = view(reg_b, 4608, FD)
        early = view(reg_y, 0, D_N)
        w_bd = view(reg_y, 1408, 2, P)
        m_cs = view(reg_b, 4864, 2, 2, P)
        bc = view(reg_b, 0, 6, D)
        g2bc = view(reg_b, 0, 2, D)
        nfbc = view(reg_b, 2048, D)
        h2t = view(reg_p, 0, KD, NTOK)
        eq_ke = view(reg_p, 5120, TOPK, E)
        a_oh = [view(reg_p, 5632, TOPK, P), view(reg_b, 5120, TOPK, P)]
        eq_tmp = view(reg_p, 6656, TOPK, E)
        x2_tmp = view(reg_p, 5632, D)
        dg2 = view(reg_p, 5632, 2, 4, P)
        up_early, up_late = view(reg_h, 0, 2, F), view(reg_b, 3072, 2, F)
        sh_out = view(reg_h, 2048, 2, D)
        h2row = view(reg_y, 0, 2, D)
        b_oh = [view(reg_y, 0, TOPK, 2, NT), view(reg_h, 0, TOPK, 2, NT)]
        xg = view(reg_h, 0, 2, D)
        xg_t = view(reg_h, 2048, 2, KD * P)
        sg = view(reg_h, 4096, 2, F)
        hh = view(reg_h, 4608, 2, F)
        yb = view(reg_y, 0, 2, D)
        h_t = view(reg_y, 2048, 2, 2 * P)

        def shared_rows(t):
            return sh_out[:, 1 if t == T - 1 else t % 2, :]

        keep = sb("keep", [P, C_N])
        ident, ones, iota = keep[:, C_ID:C_ID + P], keep[:, C_ONE:C_ONE + P], keep[:, C_IOTA:C_IOTA + P]
        identb = sb("identb", [P, P], BF16)
        onesb = sb("onesb", [P, P], BF16)
        upper = sb("upper", [P, P], BF16)
        maskb = sb("maskb", [P, 2, P], BF16)
        cv = sb("cv", [P, 2, KD])
        cw = sb("cw", [P, 2, KD])
        silu_c = sb("silu_c", [P, 2, KD])
        bmod = sb("bmod", [P, 6, KD])
        nrm = sb("nrm", [P, 2, KD])
        mod = sb("mod", [P, 6, KD, 2])
        a1 = sb("a1", [P, KD, 2])
        a2 = sb("a2", [P, KD, 2])
        dg = view(ring, s3, 2, 4, P)
        mod_acc = [(view(ring, s3 + 2048, D), view(ring, s3 + 3072, D)), (view(reg_b, 1536, D), view(reg_p, 6656, D))]
        nsink = sb("nsink", [P, NH])
        psink = sb("psink", [P, NH])
        ssq = sb("ssq", [P, 3 * T])
        rstd = sb("rstd", [P, 3 * T])
        mx = sb("mx", [P, 2])
        negm = sb("negm", [P, 2, NH])
        rsum = sb("rsum", [P, 2, NH])
        den = sb("den", [P, 2, 6])
        wr = view(reg_y, 2048, KD, E)
        rbias = sb("rbias", [P, E])
        sig = view(reg_p, 7168, T, E)
        sc = view(reg_p, 7584, E)
        g8 = view(reg_p, 7488, 8, 8)
        gsc = sb("gsc", [P, 8])
        top = sb("top", [P, 8])
        topi = sb("topi", [P, 8], U32)
        gif = sb("gif", [P, 8])
        geq = view(reg_p, 7552, 8, 4)
        gpen = sb("gpen", [P, 8])
        eif = sb("eif", [P, T, TOPK])
        gate = sb("gate", [P, T, TOPK])
        gsum = sb("gsum", [P, 2])
        maskm = sb("maskm", [P, T, E], BF16)
        xb = view(reg_b, 4704, E)
        xinc = view(reg_b, 4768, E)
        blk = view(reg_b, 3904, T, E)
        jmap = view(reg_b, 4224, T, E)
        code = view(reg_b, 4944, T, TOPK)
        place_f = view(reg_b, 4984, T, TOPK)
        block_f = view(reg_b, 5024, T, TOPK)
        row_f = view(reg_b, 5064, T, TOPK)
        eps = sb("eps", [P, 1])
        tripf = sb("tripf", [1, 32])
        tripn = sb("tripn", [1, 2])
        trip = sb("trip", [1, 2], I32)
        eidf = reg_b[0:1, 4832:4832 + NT]
        eid = sb("eid", [1, NT], I32)
        row_i = sb("row_i", [P, NT], U32)
        tok_i = sb("tok_i", [P, NT], U32)
        gate_s = sb("gate_s", [P, NT])
        tokc = sb("tokc", [P, 2], U32)
        rowc = sb("rowc", [P, 2], U32)

        bank = [ctx.enter_context(nc.psum_tensor(f"bank{i}", [P, 512], F32)) for i in range(8)]

        s_c = sem("conditions_in")
        s_small = sem("small_inputs_in")
        s_x = sem("tokens_in")
        s_late = sem("attention_inputs_in")
        s_wf = sem("fourier_weights_in")
        s_late2 = sem("router_inputs_in")
        s_ring = [sem(f"ring_slot{i}_in") for i in range(4)]
        s_ac = sem("act_chain")
        s_dv = sem("dve_chain")
        s_cexp = sem("c_exp")
        s_silu = sem("silu_c_ready")
        s_modpe = sem("mod_section_summed")
        s_modv = sem("mod_section_ready")
        s_piece = [sem(f"mod_piece_in{i}") for i in range(9)]
        s_md = sem("mod_piece_by_dve")
        s_ma = sem("mod_piece_scaled_by_act")
        s_mp0 = sem("mod_piece_half_by_pool")
        s_mp = sem("mod_piece_by_pool")
        s_ssq = sem("square_sums")
        s_std = sem("std")
        s_xh = sem("xhat_ready")
        s_tr = sem("xhat_transposed")
        s_h1a = sem("h1t_by_act")
        s_h1b = sem("h1t_by_dve")
        s_pa = sem("proj_even_group_done")
        s_pb = sem("proj_odd_group_done")
        s_ea = sem("proj_evacuated_by_act")
        s_eb = sem("proj_evacuated_by_dve")
        s_rot = sem("rotated")
        s_qk = sem("qk_transposed")
        s_qa = sem("qk_t_by_act")
        s_qb = sem("qk_t_by_dve")
        s_cst = sem("bf16_constants_ready")
        s_wbd0 = sem("w_blockdiag_cleared")
        s_m = sem("dft_w_done")
        s_me = sem("dft_w_ready")
        s_f = sem("fourier_pe")
        s_fa = sem("fourier_by_act")
        s_fb = sem("fourier_by_dve")
        s_s = sem("scores_done")
        s_nm = sem("neg_max_ready")
        s_ex = sem("probs_ready")
        s_pt = sem("probs_transposed")
        s_pta = sem("probs_t_by_act")
        s_ptb = sem("probs_t_by_dve")
        s_pvu = sem("pv_done")
        s_nk = sem("new_kv_out")
        s_se = sem("sink_exp_in")
        s_sx = sem("sink_exp_ready")
        s_on = sem("attn_out_normed")
        s_mt = sem("mix_transposed")
        s_mta = sem("mix_t_ready")
        s_dg = sem("diag_ready")
        s_bp = sem("broadcast_pe")
        s_ba = sem("broadcast_ready")
        s_op = sem("outproj_done")
        s_x2 = sem("outproj_read")
        s_x2r = sem("x2_ready")
        s_sq2 = sem("x2_squares")
        s_st2 = sem("x2_std")
        s_h2a = sem("h2_rows_scaled")
        s_h2 = sem("h2_rows_ready")
        s_h2o = [sem(f"h2_rows_out{i}") for i in range(2)]
        s_t2 = sem("h2_transposed")
        s_t2a = sem("h2t_by_act")
        s_t2b = sem("h2t_by_dve")
        s_r = sem("logits_done")
        s_re = sem("logit_exp_ready")
        s_rs = sem("sigmoid_ready")
        s_mm = sem("expert_mask_ready")
        s_pos = sem("positions_done")
        s_oh = sem("onehots_ready")
        s_tb = sem("table_tile_done")
        s_tab = sem("tables_ready")
        s_trip = sem("block_count_ready")
        s_eps = sem("eps_ready")
        s_shg = sem("shared_gu_done")
        s_shs = sem("shared_silu_ready")
        s_shh = sem("shared_h_ready")
        s_sht = sem("shared_h_transposed")
        s_she = sem("shared_h_t_ready")
        s_shd = sem("shared_down_done")
        s_sho = sem("shared_out_copied")
        s_shm = sem("shared_gated")
        s_shx = sem("shared_added")
        s_xg = [sem(f"gathered{i}") for i in range(2)]
        s_idx = sem("pool_index_copied")
        s_pool = sem("pool_wait_passed")
        s_xt = sem("block_transposed")
        s_xa = sem("block_t_by_act")
        s_xb = sem("block_t_by_dve")
        s_g = sem("block_gate_up_done")
        s_sg = sem("block_silu_ready")
        s_h = sem("block_h_ready")
        s_ht = sem("block_h_transposed")
        s_he = sem("block_h_t_ready")
        s_y = sem("block_down_done")
        s_ya = sem("block_y_by_act")
        s_yb = sem("block_y_by_dve")
        s_yo = [sem(f"scattered{i}") for i in range(2)]
        s_g0 = sem("gather_buffers_cleared")
        s_row = [sem(f"token_rows_in{i}") for i in range(6)]
        s_fr = sem("token_rows_read")
        s_x3 = sem("x3_ready")
        s_sq3 = sem("x3_squares")
        s_st3 = sem("x3_std")
        s_fin = sem("outputs_ready")
        s_out = sem("outputs_out")
        s_nf = sem("final_norm_in")
        block = ctx.enter_context(nc.Block())

        items = [("pieces", 0, 0), ("win", 0, 1), ("win", 1, 0), ("pieces", 1, 2), ("dft", 0, 2), ("wout", 0, 0),
                 ("wout", 1, 1)]
        whole = [it for it in items if it[0] != "pieces"]
        uses = [sum(1 for it in whole if it[2] == s) for s in range(4)]
        nth = {it[:2]: sum(1 for o in whole[:n + 1] if o[2] == it[2]) for n, it in enumerate(whole)}
        where = {it[:2]: it[2] for it in items}
        last_use = {"win": (s_pb, 2 * T), "pieces": (s_mp, PIECES - 4), "dft": (s_f, 7)}

        def section_of(i):
            return (i % 2, i // 2) if i < 8 else (2 + (i - 8) // 4, (i - 8) % 4)

        def scaled_before(i):
            return i // 2 if i < 8 else i - 4

        def piece(i):
            s, third = ((1, 0)[i // 3], i % 3) if i < 6 else (2, i % 3)
            return view(ring, slot(s) + 2048 * third, 2, D)

        def piece_in(i):
            return (s_piece[i], 16) if i < 6 else (s_piece[6 + i % 3], 16 * (i // 3 - 1))

        def piece_read(eng, i):
            if section_of(i)[0] == 0:
                eng.wait_ge(s_md, i + 1)
            else:
                eng.wait_ge(s_mp, scaled_before(i) + 1)

        def arrived(eng, what, n):
            eng.wait_ge(s_ring[where[what, n]], 16 * nth[what, n])

        def item_slot(m):
            return (m + 2) % 4

        def experts_in(m_div, s):
            return 16 * uses[s] + 48 * (m_div + 1)

        def at_least(eng, s, value):
            if not isinstance(value, int) or value > 0:
                eng.wait_ge(s, value)

        def w_gu(s):
            return ring[:, slot(s):slot(s) + 4096].rearrange("p (w k f) -> p k w f", w=2, k=KD)

        def w_dn(s):
            return ring[:, slot(s) + 4096:slot(s) + SLOT].rearrange("p (k n) -> p k n", k=2)

        def load_expert(eng, s, gate_ap, up_ap, down_ap):
            o = slot(s)
            eng.dma_start(ring[:, o:o + 2048], gate_ap).then_inc(s_ring[s], 16)
            eng.dma_start(ring[:, o + 2048:o + 4096], up_ap).then_inc(s_ring[s], 16)
            eng.dma_start(ring[:, o + 4096:o + 6144], down_ap).then_inc(s_ring[s], 16)

        wg_v = w_gate.rearrange("l e (p k) f -> (l e) p (k f)", p=P)
        wu_v = w_up.rearrange("l e (p k) f -> (l e) p (k f)", p=P)
        wd_v = w_down.rearrange("l e (p k) n -> (l e) p (k n)", p=P)
        wmod_v = w_mod[0].rearrange("(p k) n -> p k n", p=P)
        win_v = w_in[0].rearrange("(p k) n -> p k n", p=P)
        wout_v = w_out[0].rearrange("(k p) n -> p k n", p=P)

        @block.sync
        def _(sp):
            sp.dma_start(cv[:, 0, :], c_ctx.rearrange("(p k) -> p k", p=P)).then_inc(s_c, 16)
            sp.dma_start(cv[:, 1, :], c[0].rearrange("(p k) -> p k", p=P)).then_inc(s_c, 16)
            def mod_pieces(first, end):
                for i in range(first, end):
                    if i >= 9:
                        piece_read(sp, i - 3)
                    sec, j = section_of(i)
                    sp.dma_start(piece(i), wmod_v[:, 2 * j:2 * j + 2, sec * D:(sec + 1) * D]).then_inc(piece_in(i)[0], 16)

            before = {}
            for what, n, s in items:
                if what == "win":
                    for i in range(3 * n, 3 * n + 3):
                        piece_read(sp, i)
                elif s in before:
                    sm, v = last_use[before[s]]
                    sp.wait_ge(sm, v)
                before[s] = what
                o = slot(s)
                if what == "pieces":
                    mod_pieces(*((0, 9), (9, PIECES))[n])
                elif what == "win":
                    sp.dma_start(view(ring, o, 4, PROJ), win_v[:, 4 * n:4 * n + 4, :]).then_inc(s_ring[s], 16)
                elif what == "dft":
                    sp.dma_start(ring[:, o:o + 4096], dft_c).then_inc(s_ring[s], 16)
                else:
                    sp.dma_start(view(ring, o, 4, D), wout_v[:, 4 * n:4 * n + 4, :]).then_inc(s_ring[s], 16)
            sp.wait_ge(s_f, 7)
            load_expert(sp, 2, ws_gate[0].rearrange("(p k) f -> p (k f)", p=P),
                        ws_up[0].rearrange("(p k) f -> p (k f)", p=P),
                        ws_down[0].rearrange("(p k) n -> p (k n)", p=P))
            sp.wait_ge(s_bp, 12)
            load_expert(sp, 3, wg_v[0], wu_v[0], wd_v[0])
            sp.wait_ge(s_op, 2 * T)
            load_expert(sp, 0, wg_v[1], wu_v[1], wd_v[1])
            load_expert(sp, 1, wg_v[2], wu_v[2], wd_v[2])
            sp.wait_ge(s_shd, T)
            load_expert(sp, 2, wg_v[3], wu_v[3], wd_v[3])
            sp.wait_ge(s_trip, 1)
            last_p = sp.value_load(trip[0:1, 0:1], min_val=E // 2 - 1, max_val=2 * GROUPS - 1)
            with sp.Fori(1, GROUPS) as i:
                for half in range(2):
                    with sp.If(i * 2 + half < last_p + 1):
                        for j in range(2 * half, 2 * half + 2):
                            e = sp.value_load(eid[0:1, bass.ds(i * 4 + j, 1)], min_val=0, max_val=E - 1)
                            sp.wait_ge(s_y, i * 4 + j - 3)
                            load_expert(sp, item_slot(j + 1), wg_v[bass.ds(e, 1)].rearrange("e p n -> (e p) n"),
                                        wu_v[bass.ds(e, 1)].rearrange("e p n -> (e p) n"),
                                        wd_v[bass.ds(e, 1)].rearrange("e p n -> (e p) n"))
            sp.wait_ge(s_y, last_p * 2 + 2)
            sp.wait_ge(s_yo[0], last_p * 16 + 16)
            sp.wait_ge(s_yo[1], last_p * 16 + 16)
            for n in range(2 * T):
                t, half = divmod(n, 2)
                if n >= 6:
                    sp.wait_ge(s_fr, t - 2)
                sp.dma_start(ring[:, (n % 6) * 4096:(n % 6 + 1) * 4096].rearrange("p (k d) -> p k d", k=4),
                             y_dram[t * P * TOPK:(t + 1) * P * TOPK, :]
                             .rearrange("(p k) d -> p k d", k=TOPK)[:, 4 * half:4 * half + 4, :])\
                  .then_inc(s_row[n % 6], 16)
            for t in range(T):
                sp.wait_ge(s_fin, t + 1)
                dst = y_prompt[0] if t == 0 else y_sample[0, (t - 1) * P:t * P, :]
                sp.dma_start(dst, xs[:, t, :]).then_inc(s_out, 16)
            sp.wait_ge(s_out, 16 * T)
            sp.wait_ge(s_nk, 32)

        @block.gpsimd
        def _(pool):
            def shared_add(pool, t):
                pool.wait_ge(s_sho, t + 1)
                out = shared_rows(t)
                pool.tensor_tensor(out, out, g2bc[:, min(t, 1), :], ALU.mult).then_inc(s_shm, 1)
                pool.wait_ge(s_shm, t + 1)
                pool.tensor_tensor(xs[:, t, :], xs[:, t, :], out, ALU.add).then_inc(s_shx, 1)

            pool.memset(eps[:], EPS).then_inc(s_eps, 1)
            pool.memset(w_bd, 0.0).then_inc(s_wbd0, 1)
            pool.wait_ge(s_wbd0, 1)
            for g in range(4):
                h = 64 * (g % 2)
                pool.dma_start(w_bd[h:h + 64, g // 2, h:h + 64], w_fourier[0, g]).then_inc(s_wf, 16)
            for i in range(PIECES):
                sec, j = section_of(i)
                if sec == 0:
                    continue
                m = scaled_before(i)
                acc = mod_acc[sec % 2][0]
                pool.wait_ge(s_ma, m + 1)
                if j:
                    pool.wait_ge(s_mp, m)
                    pool.tensor_tensor(acc, acc, piece(i)[:, 0, :], ALU.add).then_inc(s_mp0, 1)
                    pool.wait_ge(s_mp0, m + 1 - sec)
                pool.tensor_tensor(acc, acc, piece(i)[:, 1, :], ALU.add).then_inc(s_mp, 1)
            for t in range(T):
                pool.wait_ge(s_x2, 2 * t + 2)
                pool.tensor_tensor(xs[:, t, :], xs[:, t, :], x2_tmp, ALU.add).then_inc(s_x2r, 1)
                pool.wait_ge(s_h2a, t + 1)
                pool.tensor_tensor(h2row[:, t % 2, :], h2row[:, t % 2, :], bc[:, 4 + min(t, 1), :], ALU.add)\
                    .then_inc(s_h2, 1)
            def shared_h(pool, t):
                pool.wait_ge(s_shs, t + 1)
                if t >= 2:
                    pool.wait_ge(s_sht, t - 1)
                up = (up_early if t < 2 else up_late)[:, t % 2, :]
                pool.tensor_tensor(hh[:, t % 2, :], sg[:, t % 2, :], up, ALU.mult).then_inc(s_shh, 1)

            shared_h(pool, 0)
            shared_h(pool, 1)
            pool.wait_ge(s_shh, 2)
            pool.memset(xg, 0.0).then_inc(s_g0, 1)
            pool.wait_ge(s_ba, 16)
            shared_h(pool, 2)
            shared_add(pool, 0)
            shared_h(pool, 3)
            for t in range(1, T - 1):
                shared_add(pool, t)
            pool.wait_ge(s_tab, 1)
            for b in range(2):
                pool.tensor_copy(tokc[:, b:b + 1], tok_i[:, b:b + 1]).then_inc(s_idx, 1)
            pool.wait_ge(s_h2o[0], 48)
            pool.wait_ge(s_h2o[1], 32)
            pool.wait_ge(s_g0, 1)

            def gather(p):
                pool.indirect_dma_start(out=xg[:, p, :], out_offset=None, in_=h2_dram,
                                        in_offset=bass.IndirectOffsetOnAxis(ap=tokc[:, p:p + 1], axis=0),
                                        bounds_check=NTOK - 1, oob_is_err=False).then_inc(s_xg[p], 16)

            def scatter(cb, p, copied, earlier):
                at_least(pool, s_yo[p], earlier)
                pool.sem_inc(s_pool, 1)
                pool.tensor_copy(rowc[:, p:p + 1], row_i[:, bass.ds(cb, 1)]).then_inc(s_idx, 1)
                pool.wait_ge(s_ya, cb + 1)
                pool.wait_ge(s_yb, cb + 1)
                pool.wait_ge(s_idx, copied)
                pool.sem_inc(s_pool, 1)
                pool.indirect_dma_start(out=y_dram, out_offset=bass.IndirectOffsetOnAxis(ap=rowc[:, p:p + 1], axis=0),
                                        in_=yb[:, p, :], in_offset=None,
                                        bounds_check=NROW - 1, oob_is_err=False).then_inc(s_yo[p], 16)

            pool.wait_ge(s_idx, 2)
            gather(0)
            gather(1)
            shared_h(pool, T - 1)
            shared_add(pool, T - 1)

            def step(i, j):
                b, p = i * 4 + j, j % 2
                first = isinstance(b, int) and b == 0
                pool.wait_ge(s_xt, b + 1)
                pool.sem_inc(s_pool, 1)
                pool.tensor_copy(tokc[:, p:p + 1], tok_i[:, bass.ds(b + 2, 1)]).then_inc(s_idx, 1)
                pool.wait_ge(s_idx, 3 if first else b * 2 + 2)
                pool.sem_inc(s_pool, 1)
                gather(p)
                if not first:
                    scatter(b - 1, 1 - p, b * 2 + 3, i * 32 + 16 * ((j - 1) // 2))

            pool.wait_ge(s_trip, 1)
            last_p = pool.value_load(trip[0:1, 0:1], min_val=E // 2 - 1, max_val=2 * GROUPS - 1)
            for j in range(4):
                step(0, j)
            with pool.Fori(1, GROUPS) as i:
                for half in range(2):
                    with pool.If(i * 2 + half < last_p + 1):
                        for j in range(2 * half, 2 * half + 2):
                            step(i, j)
            scatter(last_p * 2 + 1, 1, last_p * 4 + 6, last_p * 16)
            pool.wait_ge(s_xg[0], last_p * 16 + 32)
            pool.wait_ge(s_xg[1], last_p * 16 + 32)

        @block.scalar
        def _(act):
            n_chain = [0]

            def link(ins):
                n_chain[0] += 1
                ins.then_inc(s_ac, 1)
                act.wait_ge(s_ac, n_chain[0])

            act.dma_start(bmod[:], b_mod[0].rearrange("(s p k) -> p s k", s=6, p=P)).then_inc(s_small, 16)
            act.dma_start(nrm[:, 0, :], norm1[0].rearrange("(p k) -> p k", p=P)).then_inc(s_small, 16)
            act.dma_start(nrm[:, 1, :], norm2[0].rearrange("(p k) -> p k", p=P)).then_inc(s_small, 16)
            act.dma_start(keep[:], keep_c).then_inc(s_small, 16)
            act.dma_start(xs[:, 0, :], x_prompt[0]).then_inc(s_x, 16)
            act.dma_start(xs[:, 1:T, :], x_sample[0].rearrange("(t p) d -> p t d", p=P)).then_inc(s_x, 16)
            act.dma_start(early, early_c).then_inc(s_late, 16)
            act.dma_start(psink[:], sink.to_broadcast([P, NH])).then_inc(s_late, 16)
            act.dma_start(kctx, cache_k[0, 0].rearrange("s h d -> s (h d)")).then_inc(s_late, 16)
            act.dma_start(v_sb[:, T, :], cache_v[0, 0].rearrange("s h d -> s (h d)")).then_inc(s_late, 16)
            act.dma_start(wr[:], w_router[0].rearrange("(p k) e -> p k e", p=P)).then_inc(s_late2, 16)
            act.dma_start(rbias[:], router_bias.to_broadcast([P, E])).then_inc(s_late2, 16)

            act.wait_ge(s_c, 32)
            act.activation(cw[:], cv[:], ACT.Exp, scale=-1.0).then_inc(s_cexp, 1)
            def mod_piece(i):
                sec, j = section_of(i)
                act.wait_ge(s_md, i + 1)
                if j == 0 and sec >= 2:
                    act.wait_ge(s_modpe, sec - 1)
                for k in range(2):
                    to = mod_acc[sec % 2][0] if j == 0 and k == 0 else piece(i)[:, k, :]
                    last = act.activation(to, piece(i)[:, k, :], ACT.Copy, scale=silu_c[:, 0, 2 * j + k:2 * j + k + 1])
                last.then_inc(s_ma, 1)

            mod_piece(1)
            mod_piece(3)
            act.wait_ge(s_x, 32)
            for t in range(T):
                last = act.activation(view(reg_p, 2816, D), xs[:, t, :], ACT.Square,
                                      accum_out=ssq[:, t:t + 1])
                if t < T - 1:
                    link(last)
            last.then_inc(s_ssq, 1)
            mod_piece(5)
            mod_piece(7)
            act.wait_ge(s_ssq, 1)
            act.wait_ge(s_eps, 1)
            act.activation(rstd[:, 0:T], ssq[:, 0:T], ACT.Sqrt, scale=1.0 / D, bias=eps[:]).then_inc(s_std, 1)

            def h1_half(t):
                act.wait_ge(s_tr, 2 * t + 1)
                if t == 0:
                    act.wait_ge(s_modv, 3)
                for k in range(4):
                    cond = min(t, 1)
                    last = act.activation(h1t[:, k, t * P:(t + 1) * P], bank[2][:, k * P:(k + 1) * P], ACT.Identity,
                                          scale=a1[:, k, cond:cond + 1], bias=mod[:, 0, k, cond:cond + 1])
                last.then_inc(s_h1a, 1)

            def q_out(t):
                act.wait_ge(s_qk, 2 * t + 1)
                act.copy(q_t[:, t, 0:4, :].rearrange("p a b -> p (a b)"), bank[6][:, :]).then_inc(s_qa, 1)

            h1_half(0)
            for t in range(T):
                if t + 1 < T:
                    h1_half(t + 1)
                act.wait_ge(s_pa, 2 * t + 1)
                if t >= 2:
                    act.wait_ge(s_rot, t - 2) if t > 2 else act.wait_ge(s_qk, 2)
                act.copy(qk[:, t % 2, 0:384], bank[4][:, 0:384]).then_inc(s_ea, 1)
                if t:
                    mod_piece(8 + 4 * t - 2)
                    mod_piece(8 + 4 * t - 1)
                act.wait_ge(s_pa, 2 * t + 2)
                act.copy(u_sb[:, t, :], bank[4][:, 0:FD]).then_inc(s_ea, 1)
                if t >= 1:
                    q_out(t - 1)
                if t + 1 < T:
                    mod_piece(8 + 4 * t)
                    mod_piece(8 + 4 * t + 1)
                if t == 0:
                    act.wait_ge(s_eb, 2)
                    act.dma_start(new_k[0, 0].rearrange("s h d -> s (h d)"), qk[:, 0, 768:1024]).then_inc(s_nk, 16)
                    act.dma_start(new_v[0, 0].rearrange("s h d -> s (h d)"), v_sb[:, 0, :]).then_inc(s_nk, 16)

            q_out(T - 1)
            act.wait_ge(s_m, 1)
            act.copy(m_cs.rearrange("p a b c -> p (a b c)"), bank[0][:, :]).then_inc(s_me, 1)
            n = 0
            for cc in range(2):
                for w0, wn in ((0, P), (P, 512)):
                    act.wait_ge(s_f, 1 + 2 * n)
                    act.copy(y_cs[:, 0, 0:wn], bank[0][:, 0:wn]).then_inc(s_fa, 1)
                    act.wait_ge(s_f, 2 + 2 * n)
                    act.copy(mix_t[:, cc, w0:w0 + wn], bank[2][:, 0:wn]).then_inc(s_fa, 1)
                    n += 1

            units = [(i, h) for i in range(T) for h in range(NH)]

            def exps(u):
                i, h = units[u]
                n_keys = keys_of(turn[i])[1]
                act.wait_ge(s_nm, u + 1)
                if u >= 2:
                    act.wait_ge(s_pt, u - 1)
                act.activation(prob[:, u % 2, 0:n_keys], bank[u % 3][:, 0:n_keys], ACT.Exp, scale=SCALE,
                               bias=negm[:, i % 2, h:h + 1], accum_out=rsum[:, i % 2, h:h + 1]).then_inc(s_ex, 1)

            def half_tile(n):
                act.wait_ge(s_se, n + 1)
                act.activation(den[:, n % 2, :], den[:, n % 2, :], ACT.Exp).then_inc(s_sx, 1)

            def mix_half(n):
                i, g = divmod(n, 2)
                t = turn[i]
                act.wait_ge(s_mt, n + 1)
                act.copy(mix_t[:, 2 + 3 * g:5 + 3 * g, t * P:(t + 1) * P],
                         bank[7][:, 0:384].rearrange("p (a b) -> p a b", a=3)).then_inc(s_mta, 1)

            exps(0)
            exps(1)
            for u in range(len(units)):
                if u % 2:
                    act.wait_ge(s_pt, u + 1)
                    n_keys = keys_of(turn[units[u][0]])[1]
                    if u >= 2:
                        act.wait_ge(s_pvu, u - 1)
                    act.copy(prob_t[:, 1, 0:n_keys], bank[4][:, 0:n_keys]).then_inc(s_pta, 1)
                if u + 2 < len(units):
                    exps(u + 2)
                if u % 6 == 0 and u:
                    half_tile(u // 6 - 1)
                if u % 6 == 3 and u > 6:
                    mix_half(u // 6 - 1)
            half_tile(9)
            mix_half(9)

            for v in range(6):
                for hf in range(2):
                    n = 2 * v + hf
                    act.wait_ge(s_bp, n + 1)
                    act.copy(bc[:, v, :].rearrange("p (q k) -> p k q", k=KD)[:, 4 * hf:4 * hf + 4, :],
                             bank[n % 2][:, :].rearrange("p (k q) -> p k q", k=4)).then_inc(s_ba, 1)

            def norm2_of(t):
                act.wait_ge(s_x2r, t + 1)
                act.activation(h2row[:, t % 2, :], xs[:, t, :], ACT.Square,
                               accum_out=ssq[:, T + t:T + t + 1]).then_inc(s_sq2, 1)
                act.wait_ge(s_sq2, t + 1)
                act.activation(rstd[:, T + t:T + t + 1], ssq[:, T + t:T + t + 1], ACT.Sqrt, scale=1.0 / D,
                               bias=eps[:]).then_inc(s_st2, 1)

            def logit_exp(t):
                act.wait_ge(s_r, t + 1)
                act.activation(sig[:, t, :], bank[6 + t % 2][:, 0:E], ACT.Exp, scale=-1.0).then_inc(s_re, 1)

            def shared_silu(t):
                act.wait_ge(s_shg, t + 1)
                if t >= 2:
                    act.wait_ge(s_shh, t - 1)
                if t == 2:
                    act.wait_ge(s_h2, T)
                act.copy((up_early if t < 2 else up_late)[:, t % 2, :], bank[2 + t % 2][:, F:2 * F])
                act.activation(sg[:, t % 2, :], bank[2 + t % 2][:, 0:F], ACT.Silu).then_inc(s_shs, 1)

            def g2_row(n):
                act.wait_ge(s_bp, 12 + n + 1)
                act.copy(g2bc[:, n // 2, :].rearrange("p (q k) -> p k q", k=KD)[:, 4 * (n % 2):4 * (n % 2) + 4, :],
                         bank[n % 2][:, :].rearrange("p (k q) -> p k q", k=4)).then_inc(s_ba, 1)

            for t in range(T):
                if t >= 2:
                    act.wait_ge(s_h2o[t % 2], 16 * (t // 2))
                    act.wait_ge(s_t2, 2 * (t - 1))
                norm2_of(t)
                if t == T - 1:
                    shared_silu(0)
                act.wait_ge(s_h2, t + 1)
                act.dma_start(h2_dram[t * P:(t + 1) * P, :], h2row[:, t % 2, :]).then_inc(s_h2o[t % 2], 16)
                if t:
                    logit_exp(t - 1)
                act.wait_ge(s_t2, 2 * t + 1)
                act.copy(h2t[:, 0:4, t * P:(t + 1) * P], bank[4][:, :].rearrange("p (a b) -> p a b", a=4)).then_inc(s_t2a, 1)
            g2_row(0)
            g2_row(1)
            logit_exp(T - 1)
            g2_row(2)
            g2_row(3)
            act.dma_start(nfbc, norm_f.rearrange("(a n) -> a n", a=1).to_broadcast([P, D])).then_inc(s_nf, 16)

            def shared_out(t):
                act.wait_ge(s_shd, t + 1)
                if t >= 2:
                    act.wait_ge(s_shx, t if t == T - 1 else t - 1)
                act.copy(shared_rows(t)[:, 0:512], bank[0][:, :])
                act.copy(shared_rows(t)[:, 512:1024], bank[1][:, :]).then_inc(s_sho, 1)

            def shared_rest(t):
                act.wait_ge(s_sht, t + 1)
                act.copy(h_t[:, t % 2, :], bank[4][:, 0:2 * P]).then_inc(s_she, 1)
                shared_out(t)

            shared_silu(1)
            shared_silu(2)
            shared_rest(0)
            shared_silu(3)
            for t in range(1, T - 1):
                shared_rest(t)
            shared_silu(T - 1)
            shared_rest(T - 1)

            def xt_half(b, p):
                act.wait_ge(s_xt, b + 1)
                act.copy(xg_t[:, p, 0:512], bank[0][:, :]).then_inc(s_xa, 1)

            def h_t_out(cb, p):
                act.wait_ge(s_ht, cb + 1)
                act.copy(h_t[:, p, :], bank[4][:, 0:2 * P]).then_inc(s_he, 1)

            def y_half(cb, p, scattered):
                act.wait_ge(s_y, cb + 1)
                at_least(act, s_yo[p], scattered)
                act.activation(yb[:, p, 0:512], bank[5][:, :], ACT.Copy, scale=gate_s[:, bass.ds(cb, 1)]).then_inc(s_ya, 1)

            act.wait_ge(s_tab, 1)
            act.wait_ge(s_shx, T - 1)
            xt_half(0, 0)

            def step(i, j):
                b, p = i * 4 + j, j % 2
                first = isinstance(b, int) and b == 0
                if not first:
                    h_t_out(b - 1, 1 - p)
                act.wait_ge(s_g, b + 1)
                at_least(act, s_h, b - 1)
                act.activation(sg[:, p, :], bank[2 + p][:, 0:F], ACT.Silu).then_inc(s_sg, 1)
                if first:
                    act.wait_ge(s_shx, T)
                xt_half(b + 1, 1 - p)
                if not first:
                    y_half(b - 1, 1 - p, i * 32 + 16 * ((j - 1) // 2))

            act.wait_ge(s_trip, 1)
            last_p = act.value_load(trip[0:1, 0:1], min_val=E // 2 - 1, max_val=2 * GROUPS - 1)
            for j in range(4):
                step(0, j)
            with act.Fori(1, GROUPS) as i:
                for half in range(2):
                    with act.If(i * 2 + half < last_p + 1):
                        for j in range(2 * half, 2 * half + 2):
                            step(i, j)
            h_t_out(last_p * 2 + 1, 1)
            y_half(last_p * 2 + 1, 1, last_p * 16)

            for t in range(T):
                act.wait_ge(s_x3, t + 1)
                act.activation(yb[:, 1, :], xs[:, t, :], ACT.Square,
                               accum_out=ssq[:, 2 * T + t:2 * T + t + 1]).then_inc(s_sq3, 1)
                act.wait_ge(s_sq3, t + 1)
                act.activation(rstd[:, 2 * T + t:2 * T + t + 1], ssq[:, 2 * T + t:2 * T + t + 1], ACT.Sqrt,
                               scale=1.0 / D, bias=eps[:]).then_inc(s_st3, 1)

        @block.vector
        def _(dve):
            n_chain = [0]

            def link(ins):
                n_chain[0] += 1
                ins.then_inc(s_dv, 1)
                dve.wait_ge(s_dv, n_chain[0])

            dve.wait_ge(s_cexp, 1)
            link(dve.tensor_scalar_add(cw[:], cw[:], 1.0))
            link(dve.reciprocal(cw[:], cw[:]))
            dve.tensor_tensor(silu_c[:], cv[:], cw[:], ALU.mult).then_inc(s_silu, 1)
            def mod_piece(i):
                sec, j = section_of(i)
                dve.wait_ge(*piece_in(i))
                if j == 0 and sec >= 2:
                    dve.wait_ge(s_modpe, sec - 1)
                for k in range(2):
                    for cond in ((0, 1) if sec == 0 else (1,)):
                        acc = mod_acc[sec % 2][cond]
                        scale = silu_c[:, cond, 2 * j + k:2 * j + k + 1]
                        if j == 0 and k == 0:
                            last = dve.tensor_scalar(acc, piece(i)[:, k, :], scale, None, ALU.mult)
                        else:
                            last = dve.scalar_tensor_tensor(acc, piece(i)[:, k, :], scale, acc, ALU.mult, ALU.add)
                    if k == 0:
                        link(last)
                last.then_inc(s_md, 1)
                dve.wait_ge(s_md, i + 1)

            dve.wait_ge(s_silu, 1)
            for i in range(8):
                mod_piece(i)
            dve.wait_ge(s_small, 64)
            dve.tensor_copy(identb[:], ident)
            dve.tensor_copy(onesb[:], ones)

            def section(s):
                dve.wait_ge(s_modpe, s + 1)
                src = bank[s % 2][:, 0:2 * KD].rearrange("p (k c) -> p k c", c=2)
                dve.tensor_tensor(mod[:, s], src, bmod[:, s, :].unsqueeze(2).to_broadcast([P, KD, 2]), ALU.add)\
                   .then_inc(s_modv, 1)

            dve.wait_ge(s_std, 1)
            link(dve.reciprocal(rstd[:, 0:T], rstd[:, 0:T]))

            def xhat(t):
                if t >= 2:
                    dve.wait_ge(s_tr, 2 * (t - 1))
                dve.tensor_scalar(xh[:, t % 2, :], xs[:, t, :], rstd[:, t:t + 1], None, ALU.mult).then_inc(s_xh, 1)

            xhat(0)
            xhat(1)
            section(0)
            section(1)
            dve.wait_ge(s_modv, 2)
            link(dve.tensor_scalar_add(a1[:], mod[:, 1], 1.0))
            dve.tensor_tensor(a1[:], a1[:], nrm[:, 0, :].unsqueeze(2).to_broadcast([P, KD, 2]), ALU.mult)\
               .then_inc(s_modv, 1)

            def h1_half(t):
                dve.wait_ge(s_tr, 2 * t + 2)
                if t == 0:
                    dve.wait_ge(s_modv, 3)
                for k in range(4, 8):
                    cond = min(t, 1)
                    last = dve.tensor_scalar(h1t[:, k, t * P:(t + 1) * P], bank[3][:, (k - 4) * P:(k - 3) * P],
                                             a1[:, k, cond:cond + 1], mod[:, 0, k, cond:cond + 1], ALU.mult, ALU.add)
                last.then_inc(s_h1b, 1)

            def qk_out(t):
                dve.wait_ge(s_qk, 2 * t + 2)
                kt = 5 if t == 0 else t - 1
                dve.tensor_copy(q_t[:, t, 4:6, :].rearrange("p a b -> p (a b)"), bank[7][:, 0:256])
                dve.tensor_copy(k_t[:, :, kt * P:(kt + 1) * P],
                                bank[7][:, 256:512].rearrange("p (a b) -> p a b", a=2)).then_inc(s_qb, 1)

            h1_half(0)
            xhat(2)
            for t in range(T):
                if t + 1 < T:
                    h1_half(t + 1)
                if t + 3 < T:
                    xhat(t + 3)
                if t:
                    mod_piece(8 + 4 * t - 2)
                if t == 0:
                    dve.wait_ge(s_late, 64)
                    dve.tensor_copy(upper[:], early[:, D_U:D_U + P])
                    dve.tensor_copy(maskb[:].rearrange("p a b -> p (a b)"), early[:, D_ML:D_ML + 2 * P]).then_inc(s_cst, 1)
                    link(dve.tensor_scalar(nsink[:], psink[:], -1.0, None, ALU.mult))
                dve.wait_ge(s_pb, 2 * t + 1)
                if t == 2:
                    dve.wait_ge(s_qk, 2)
                    dve.wait_ge(s_nk, 32)
                if t > 2:
                    dve.wait_ge(s_rot, t - 2)
                dve.tensor_copy(qk[:, t % 2, 384:768], bank[5][:, 0:384]).then_inc(s_eb, 1)
                if t:
                    mod_piece(8 + 4 * t - 1)
                dve.wait_ge(s_pb, 2 * t + 2)
                dve.tensor_copy(v_sb[:, t, :], bank[5][:, FD:2 * FD])
                dve.tensor_copy(qk[:, t % 2, 768:1024], bank[5][:, 0:FD]).then_inc(s_eb, 1)
                if t >= 1:
                    qk_out(t - 1)
                    dve.wait_ge(s_ea, 2 * t + 1)
                    dve.wait_ge(s_eb, 2 * t + 2)
                    src = qk[:, t % 2, :].rearrange("p (g x d) -> p g x d", g=32, x=2)
                    o = D_ROPE + (t - 1) * 128
                    cos = early[:, o:o + 64].unsqueeze(1).to_broadcast([P, 16, 64])
                    dve.tensor_tensor(rq.rearrange("p (h d) -> p h d", h=16),
                                      qk[:, t % 2, :].rearrange("p (h d) -> p h d", h=16), cos, ALU.mult)
                    dst = rtmp.rearrange("p (g x d) -> p g x d", g=32, x=2)
                    for s in range(2):
                        for x in range(2):
                            sin = early[:, o + 64 + 32 * s + 16 * x:o + 80 + 32 * s + 16 * x]
                            last = dve.tensor_tensor(dst[:, s::2, x, :], src[:, s::2, 1 - x, :],
                                                     sin.unsqueeze(1).to_broadcast([P, 16, 16]), ALU.mult)
                    link(last)
                    dve.tensor_tensor(rq, rq, rtmp, ALU.add).then_inc(s_rot, 1)
                if t + 1 < T:
                    mod_piece(8 + 4 * t)
                    mod_piece(8 + 4 * t + 1)
                if t:
                    section(1 + t)
            qk_out(T - 1)
            dve.wait_ge(s_qk, 2 * T + 1)
            dve.tensor_copy(k_t[:, :, 4 * P:5 * P], bank[6][:, 0:256].rearrange("p (a b) -> p a b", a=2)).then_inc(s_qb, 1)
            dve.wait_ge(s_modv, 7)
            link(dve.tensor_scalar_add(a2[:], mod[:, 4], 1.0))
            link(dve.tensor_tensor(a2[:], a2[:], nrm[:, 1, :].unsqueeze(2).to_broadcast([P, KD, 2]), ALU.mult))

            n = 0
            for cc in range(2):
                for w0, wn in ((0, P), (P, 512)):
                    dve.wait_ge(s_f, 1 + 2 * n)
                    dve.tensor_copy(y_cs[:, 1, 0:wn], bank[1][:, 0:wn]).then_inc(s_fb, 1)
                    n += 1

            units = [(i, h) for i in range(T) for h in range(NH)]

            def maxima(u):
                i, h = units[u]
                n_keys = keys_of(turn[i])[1]
                dve.wait_ge(s_s, u + 1)
                link(dve.reduce_max(mx[:, u % 2:u % 2 + 1], bank[u % 3][:, 0:n_keys], AX))
                if h == 0 and i >= 2:
                    dve.wait_ge(s_on, 2 * (i - 1))
                dve.tensor_scalar(negm[:, i % 2, h:h + 1], mx[:, u % 2:u % 2 + 1], -SCALE, nsink[:, h:h + 1],
                                  ALU.mult, ALU.min).then_inc(s_nm, 1)

            def half_tile(n):
                i, g = divmod(n, 2)
                hs = slice(6 * g, 6 * g + 6)
                dve.wait_ge(s_nm, 6 * n + 6)
                dve.tensor_tensor(den[:, n % 2, :], negm[:, i % 2, hs], psink[:, hs], ALU.add).then_inc(s_se, 1)

            def half_tile_out(n):
                i, g = divmod(n, 2)
                hs = slice(6 * g, 6 * g + 6)
                dve.wait_ge(s_sx, n + 1)
                dve.wait_ge(s_ex, 6 * n + 6)
                link(dve.tensor_tensor(den[:, n % 2, :], den[:, n % 2, :], rsum[:, i % 2, hs], ALU.add))
                link(dve.reciprocal(den[:, n % 2, :], den[:, n % 2, :]))
                dve.wait_ge(s_pvu, 6 * n + 6)
                if n >= 2:
                    dve.wait_ge(s_mt, n - 1)
                dve.tensor_tensor(on[:, n % 2, :].rearrange("p (h d) -> p h d", h=6),
                                  bank[5 + n % 2][:, 0:384].rearrange("p (h d) -> p h d", h=6),
                                  den[:, n % 2, :].unsqueeze(2).to_broadcast([P, 6, HD]), ALU.mult).then_inc(s_on, 1)

            maxima(0)
            maxima(1)
            for u in range(len(units)):
                if u + 2 < len(units):
                    maxima(u + 2)
                if u % 2 == 0:
                    dve.wait_ge(s_pt, u + 1)
                    n_keys = keys_of(turn[units[u][0]])[1]
                    if u >= 2:
                        dve.wait_ge(s_pvu, u - 1)
                    dve.tensor_copy(prob_t[:, 0, 0:n_keys], bank[3][:, 0:n_keys]).then_inc(s_ptb, 1)
                if u % 6 == 0 and u:
                    half_tile(u // 6 - 1)
                if u % 6 == 1 and u > 6:
                    half_tile_out(u // 6 - 1)
            half_tile(9)
            half_tile_out(9)

            def diagonals(n, col):
                if n >= 2:
                    dve.wait_ge(s_bp, n - 1)
                dve.tensor_tensor(dg[:, n % 2], ident.unsqueeze(1).to_broadcast([P, 4, P]),
                                  col.unsqueeze(2).to_broadcast([P, 4, P]), ALU.mult).then_inc(s_dg, 1)

            dve.wait_ge(s_ex, len(units))
            for v in range(6):
                col = (mod[:, 2], a2[:], mod[:, 3])[v // 2]
                for hf in range(2):
                    diagonals(2 * v + hf, col[:, 4 * hf:4 * hf + 4, v % 2])

            def h2t_half(t):
                dve.wait_ge(s_t2, 2 * t + 2)
                dve.tensor_copy(h2t[:, 4:8, t * P:(t + 1) * P], bank[5][:, :].rearrange("p (a b) -> p a b", a=4))\
                   .then_inc(s_t2b, 1)

            def route(t):
                sg_t = sig[:, t, :]
                dve.wait_ge(s_re, t + 1)
                link(dve.tensor_scalar_add(sg_t, sg_t, 1.0))
                link(dve.reciprocal(sg_t, sg_t))
                link(dve.tensor_tensor(sc[:], sg_t, rbias[:], ALU.add))
                for g in range(8):
                    last = dve.max(g8[:, g, :], sc[:, 8 * g:8 * g + 8])
                link(last)
                link(dve.tensor_tensor(gsc[:], g8[:, :, 0], g8[:, :, 1], ALU.add))
                link(dve.max(top[:], gsc[:]))
                link(dve.max_index(topi[:], top[:], gsc[:]))
                link(dve.tensor_copy(gif[:], topi[:]))
                link(dve.tensor_tensor(geq[:], iota[:, 0:8].unsqueeze(2).to_broadcast([P, 8, 4]),
                                       gif[:, 0:4].unsqueeze(1).to_broadcast([P, 8, 4]), ALU.is_equal))
                link(dve.tensor_reduce(gpen[:], geq[:], AX, ALU.add))
                link(dve.tensor_scalar(gpen[:], gpen[:], -1.0, -NEG, ALU.add, ALU.mult))
                link(dve.tensor_tensor(sc[:].rearrange("p (g e) -> p g e", g=8), sc[:].rearrange("p (g e) -> p g e", g=8),
                                       gpen[:].unsqueeze(2).to_broadcast([P, 8, 8]), ALU.add))
                link(dve.max(top[:], sc[:]))
                link(dve.max_index(topi[:], top[:], sc[:]))
                link(dve.tensor_copy(eif[:, t, :], topi[:]))
                link(dve.tensor_tensor(eq_ke, iota[:, 0:E].unsqueeze(1).to_broadcast([P, TOPK, E]),
                                       eif[:, t, :].unsqueeze(2).to_broadcast([P, TOPK, E]), ALU.is_equal))
                with nc.allow_low_precision("zeros and ones are exact"):
                    dve.tensor_reduce(maskm[:, t, :], eq_ke.rearrange("p k e -> p e k"), AX, ALU.add).then_inc(s_mm, 1)
                link(dve.tensor_tensor(eq_tmp, eq_ke, sg_t.unsqueeze(1).to_broadcast([P, TOPK, E]), ALU.mult))
                link(dve.tensor_reduce(gate[:, t, :], eq_tmp, AX, ALU.add))
                link(dve.tensor_reduce(gsum[:, 0:1], gate[:, t, :], AX, ALU.add))
                link(dve.reciprocal(gsum[:, 1:2], gsum[:, 0:1]))
                dve.tensor_scalar(gate[:, t, :], gate[:, t, :], gsum[:, 1:2], ROUTED, ALU.mult, ALU.mult).then_inc(s_rs, 1)

            def g2_diagonals(cond):
                for m in range(2):
                    if cond:
                        dve.wait_ge(s_bp, 12 + m + 1)
                    dve.tensor_tensor(dg2[:, m], ident.unsqueeze(1).to_broadcast([P, 4, P]),
                                      mod[:, 5, 4 * m:4 * m + 4, cond].unsqueeze(2).to_broadcast([P, 4, P]), ALU.mult)\
                       .then_inc(s_dg, 1)

            dve.wait_ge(s_ba, 12)
            dve.wait_ge(s_late2, 32)
            for t in range(T):
                cond = min(t, 1)
                for hf in range(2):
                    dve.wait_ge(s_op, 2 * t + hf + 1)
                    if t:
                        dve.wait_ge(s_x2r, t)
                    cols = slice(512 * hf, 512 * hf + 512)
                    dve.tensor_tensor(x2_tmp[:, cols], bank[2 * (t % 2) + hf][:, :], bc[:, cond, cols], ALU.mult)\
                       .then_inc(s_x2, 1)
                if t:
                    h2t_half(t - 1)
                r = slice(T + t, T + t + 1)
                dve.wait_ge(s_st2, t + 1)
                link(dve.reciprocal(rstd[:, r], rstd[:, r]))
                dve.scalar_tensor_tensor(h2row[:, t % 2, :], xs[:, t, :], rstd[:, r], bc[:, 2 + cond, :],
                                         ALU.mult, ALU.mult).then_inc(s_h2a, 1)
                if t == T - 1:
                    h2t_half(t)
                    dve.wait_ge(s_x2r, T)
                    g2_diagonals(0)
                if t == T - 1:
                    route(T - 3)
                    g2_diagonals(1)
                if t and t != T - 2:
                    route(t - 1)
            route(T - 1)

            dve.wait_ge(s_h2, T)
            dve.wait_ge(s_pos, 1)
            dve.wait_ge(s_rs, T)
            pos, cnt = bank[6][:, 0:T * E], bank[7][:, 0:E]
            blk2, jm2 = blk[:].rearrange("p t e -> p (t e)"), jmap[:].rearrange("p t e -> p (t e)")
            link(dve.tensor_scalar(xb[:], cnt, float(P), None, ALU.is_gt))
            link(dve.tensor_scalar(blk2, pos, float(P), None, ALU.is_ge))
            for m in range(2, T):
                link(dve.scalar_tensor_tensor(xb[:], cnt, float(m * P), xb[:], ALU.is_gt, ALU.add))
                link(dve.scalar_tensor_tensor(blk2, pos, float(m * P), blk2, ALU.is_ge, ALU.add))
            link(dve.tensor_tensor_scan(xinc[:], ones[:, 0:E], xb[:], 0.0, ALU.mult, ALU.add))
            link(dve.tensor_tensor(xb[:], xinc[:], xb[:], ALU.subtract))
            link(dve.scalar_tensor_tensor(xb[:], xb[:], float(E - 1), iota[:, 0:E], ALU.add, ALU.subtract))
            link(dve.tensor_tensor(jmap[:], blk[:], xb[:].unsqueeze(1).to_broadcast([P, T, E]), ALU.add))
            link(dve.scalar_tensor_tensor(jm2, blk2, 0.0, jm2, ALU.is_gt, ALU.mult))
            link(dve.tensor_tensor(jmap[:], jmap[:], iota[:, 0:E].unsqueeze(1).to_broadcast([P, T, E]), ALU.add))
            link(dve.tensor_scalar(blk2, blk2, -float(P), None, ALU.mult))
            link(dve.tensor_tensor(blk2, blk2, pos, ALU.add))
            link(dve.scalar_tensor_tensor(jm2, jm2, float(P), blk2, ALU.mult, ALU.add))
            for t in range(T):
                link(dve.tensor_tensor(eq_ke, iota[:, 0:E].unsqueeze(1).to_broadcast([P, TOPK, E]),
                                       eif[:, t, :].unsqueeze(2).to_broadcast([P, TOPK, E]), ALU.is_equal))
                link(dve.tensor_tensor(eq_tmp, eq_ke, jmap[:, t, :].unsqueeze(1).to_broadcast([P, TOPK, E]), ALU.mult))
                link(dve.tensor_reduce(code[:, t, :], eq_tmp, AX, ALU.add))
            flat = "p t k -> p (t k)"
            code_i, part_i = row_i[:, 0:T * TOPK], tok_i[:, 0:T * TOPK]
            link(dve.tensor_copy(code_i, code.rearrange(flat)))
            link(dve.tensor_single_scalar(part_i, code_i, P - 1, ALU.bitwise_and))
            link(dve.tensor_copy(place_f.rearrange(flat), part_i))
            link(dve.tensor_single_scalar(part_i, code_i, 7, ALU.logical_shift_right))
            dve.tensor_copy(block_f.rearrange(flat), part_i)
            link(dve.tensor_tensor(row_f, iota[:, 0:TOPK].unsqueeze(1).to_broadcast([P, T, TOPK]),
                                   keep[:, C_VT:C_VT + T].unsqueeze(2).to_broadcast([P, T, TOPK]), ALU.add))
            dve.wait_ge(s_h2o[0], 48)
            dve.wait_ge(s_h2o[1], 32)
            dve.wait_ge(s_g0, 1)
            for t in range(T):
                place, blocks = a_oh[t % 2], b_oh[t % 2]
                if t >= 2:
                    dve.wait_ge(s_tb, t - 1)
                dve.tensor_tensor(place, iota.unsqueeze(1).to_broadcast([P, TOPK, P]),
                                  place_f[:, t, :].unsqueeze(2).to_broadcast([P, TOPK, P]), ALU.is_equal)
                link(dve.tensor_tensor(blocks[:, :, 1, :], iota[:, 0:NT].unsqueeze(1).to_broadcast([P, TOPK, NT]),
                                       block_f[:, t, :].unsqueeze(2).to_broadcast([P, TOPK, NT]), ALU.is_equal))
                link(dve.tensor_tensor(blocks[:, :, 0, :], blocks[:, :, 1, :],
                                       row_f[:, t, :].unsqueeze(2).to_broadcast([P, TOPK, NT]), ALU.mult))
                dve.tensor_tensor(blocks[:, :, 1, :], blocks[:, :, 1, :],
                                  gate[:, t, :].unsqueeze(2).to_broadcast([P, TOPK, NT]), ALU.mult).then_inc(s_oh, 1)
                q0 = XBLK // T * t
                link(dve.tensor_tensor(eq_tmp[0:1], xinc[0:1, :].unsqueeze(1).to_broadcast([1, 8, E]),
                                       iota[0:1, q0:q0 + 8].unsqueeze(2).to_broadcast([1, 8, E]), ALU.is_le))
                link(dve.tensor_reduce(eidf[0:1, E + q0:E + q0 + 8], eq_tmp[0:1], AX, ALU.add))
            dve.wait_ge(s_tb, T)
            link(dve.tensor_scalar(row_i[:], bank[6][:, 0:NT], float(NROW), None, ALU.add))
            link(dve.tensor_copy(gate_s[:], bank[6][:, NT:2 * NT]))
            dve.tensor_single_scalar(tok_i[:], row_i[:], 3, ALU.logical_shift_right).then_inc(s_tab, 1)
            link(dve.tensor_scalar(tripf[:], iota[0:1, 0:32], 2.0, xinc[0:1, E - 1:E], ALU.mult, ALU.is_lt))
            link(dve.tensor_reduce(tripn[:, 0:1], tripf[:], AX, ALU.add))
            link(dve.tensor_scalar(tripn[:, 0:1], tripn[:, 0:1], float(E // 2 - 1), None, ALU.add))
            link(dve.tensor_copy(trip[:, 0:1], tripn[:, 0:1]))
            dve.tensor_single_scalar(trip[:, 1:2], trip[:, 0:1], 1, ALU.bitwise_and)
            dve.tensor_copy(eidf[0:1, E + XBLK:NT], iota[0:1, E + XBLK:NT])
            link(dve.tensor_copy(eidf[0:1, 0:E], iota[0:1, 0:E]))
            link(dve.tensor_scalar(eidf[:], eidf[:], float(E - 1), None, ALU.min))
            dve.tensor_copy(eid[:], eidf[:]).then_inc(s_trip, 1)

            dve.wait_ge(s_tab, 1)
            dve.wait_ge(s_shx, T - 1)

            def xt_half(b, p):
                dve.wait_ge(s_xt, b + 1)
                dve.tensor_copy(xg_t[:, p, 512:1024], bank[1][:, :]).then_inc(s_xb, 1)

            def y_half(cb, p, scattered):
                dve.wait_ge(s_y, cb + 1)
                at_least(dve, s_yo[p], scattered)
                dve.tensor_scalar(yb[:, p, 512:1024], bank[6][:, :], gate_s[:, bass.ds(cb, 1)], None, ALU.mult)\
                   .then_inc(s_yb, 1)

            xt_half(0, 0)

            def step(i, j):
                b, p = i * 4 + j, j % 2
                dve.wait_ge(s_sg, b + 1)
                at_least(dve, s_ht, b - 1)
                dve.tensor_tensor(hh[:, p, :], sg[:, p, :], bank[2 + p][:, F:2 * F], ALU.mult).then_inc(s_h, 1)
                if isinstance(b, int) and b == 0:
                    dve.wait_ge(s_shx, T)
                xt_half(b + 1, 1 - p)
                if not (isinstance(b, int) and b == 0):
                    y_half(b - 1, 1 - p, i * 32 + 16 * ((j - 1) // 2))

            dve.wait_ge(s_trip, 1)
            last_p = dve.value_load(trip[0:1, 0:1], min_val=E // 2 - 1, max_val=2 * GROUPS - 1)
            for j in range(4):
                step(0, j)
            with dve.Fori(1, GROUPS) as i:
                for half in range(2):
                    with dve.If(i * 2 + half < last_p + 1):
                        for j in range(2 * half, 2 * half + 2):
                            step(i, j)
            y_half(last_p * 2 + 1, 1, last_p * 16)

            dve.wait_ge(s_nf, 16)
            dve.wait_ge(s_shx, T)
            for t in range(T):
                cond = min(t, 1)
                sums = []
                for n in range(2 * t, 2 * t + 2):
                    rows = ring[:, (n % 6) * 4096:(n % 6 + 1) * 4096]
                    dve.wait_ge(s_row[n % 6], 16 * (n // 6 + 1))
                    link(dve.tensor_tensor(rows[:, 0:2048], rows[:, 0:2048], rows[:, 2048:4096], ALU.add))
                    link(dve.tensor_tensor(rows[:, 0:1024], rows[:, 0:1024], rows[:, 1024:2048], ALU.add))
                    sums.append(rows[:, 0:1024])
                link(dve.tensor_tensor(sums[0], sums[0], sums[1], ALU.add))
                dve.tensor_tensor(yb[:, 0, :], sums[0], g2bc[:, cond, :], ALU.mult).then_inc(s_fr, 1)
                dve.wait_ge(s_fr, t + 1)
                dve.tensor_tensor(xs[:, t, :], xs[:, t, :], yb[:, 0, :], ALU.add).then_inc(s_x3, 1)
                r = slice(2 * T + t, 2 * T + t + 1)
                dve.wait_ge(s_st3, t + 1)
                link(dve.reciprocal(rstd[:, r], rstd[:, r]))
                dve.scalar_tensor_tensor(xs[:, t, :], xs[:, t, :], rstd[:, r], nfbc, ALU.mult, ALU.mult).then_inc(s_fin, 1)

        @block.tensor
        def _(pe):
            def xhat_t(t):
                pe.wait_ge(s_xh, t + 1)
                v = xh[:, t % 2, :].rearrange("p (q k) -> p k q", k=KD)
                for hf in range(2):
                    if t:
                        pe.wait_ge((s_h1a, s_h1b)[hf], t)
                    for k in range(4):
                        last = pe.transpose(bank[2 + hf][:, k * P:(k + 1) * P], v[:, 4 * hf + k, :], ident)
                    last.then_inc(s_tr, 1)

            def projection(t, groups):
                pe.wait_ge(s_h1a, t + 1)
                pe.wait_ge(s_h1b, t + 1)
                for g in groups:
                    if t or g >= 2:
                        pe.wait_ge((s_ea, s_eb)[g % 2], 2 * t + g // 2)
                    n = (384, 384, FD, 2 * FD)[g]
                    for k in range(KD):
                        w = view(ring, slot(where["win", k // 4]), 4, PROJ)[:, k % 4, :]
                        if g < 2:
                            rhs = w[:, FD + 384 * g:FD + 384 * (g + 1)].rearrange("p (b g d) -> p g b d", b=2, g=3)
                        else:
                            rhs = w[:, 0:FD] if g == 2 else w[:, FD + NH * HD:PROJ]
                        last = pe.matmul(bank[4 + g % 2][:, 0:n], h1t[:, k, t * P:(t + 1) * P], rhs,
                                         start=(k == 0), stop=(k == KD - 1))
                    last.then_inc((s_pa, s_pb)[g % 2], 1)

            def qk_t(t):
                if t:
                    pe.wait_ge(s_rot, t)
                    src = rq
                    pe.wait_ge(s_qa, t)
                    pe.wait_ge(s_qb, t)
                else:
                    pe.wait_ge(s_ea, 1)
                    pe.wait_ge(s_eb, 2)
                    src = qk[:, 0, :]
                for n in range(8):
                    last = pe.transpose(bank[6 + n // 4][:, (n % 4) * P:(n % 4 + 1) * P], src[:, n * P:(n + 1) * P], ident)
                    if n % 4 == 3:
                        last.then_inc(s_qk, 1)

            def mod_columns(s):
                pe.wait_ge(s_md, 7 + s if s < 2 else 8 + 4 * (s - 1))
                if s:
                    pe.wait_ge(s_mp, 4 * s)
                if s >= 2:
                    pe.wait_ge(s_modv, 3 if s < 4 else s)
                for cond in range(2):
                    v = mod_acc[s % 2][cond].rearrange("p (q o) -> p o q", o=KD)
                    for o in range(KD):
                        last = pe.matmul(bank[s % 2][:, 2 * o + cond:2 * o + cond + 1], v[:, o, :], ones[:, 0:1],
                                         start=True, stop=True)
                last.then_inc(s_modpe, 1)

            pe.wait_ge(s_small, 64)
            mod_columns(0)
            xhat_t(0)
            mod_columns(1)
            for t in range(T):
                if t + 1 < T:
                    xhat_t(t + 1)
                if t == 0:
                    arrived(pe, "win", 0)
                    arrived(pe, "win", 1)
                projection(t, (0, 1))
                projection(t, (2, 3))
                if t:
                    qk_t(t - 1)
                    mod_columns(1 + t)
            qk_t(T - 1)
            pe.wait_ge(s_qa, T)
            pe.wait_ge(s_late, 64)
            pe.wait_ge(s_wf, 64)
            for a in range(2):
                last = pe.transpose(bank[6][:, a * P:(a + 1) * P], kctx[:, a * P:(a + 1) * P], ident)
            last.then_inc(s_qk, 1)

            pe.wait_ge(s_modv, 7)
            for x, o in ((0, D_C64), (1, D_S64)):
                for cc in range(2):
                    last = pe.matmul(bank[0][:, (2 * x + cc) * P:(2 * x + cc + 1) * P], early[:, o:o + P], w_bd[:, cc, :],
                                     start=True, stop=True)
            last.then_inc(s_m, 1)
            pe.wait_ge(s_me, 1)
            pe.wait_ge(s_ea, 2 * T)
            pe.wait_ge(s_eb, 2 * T)
            arrived(pe, "dft", 0)
            dft = view(ring, slot(where["dft", 0]), LAT, 2, 512)
            n = 0
            for cc in range(2):
                for w0, wn in ((0, P), (P, 512)):
                    for x in range(2):
                        if w0 == 0:
                            o = D_DFT + x * P
                            last = pe.matmul(bank[x][:, 0:P], u_sb[:, 0, cc * P:(cc + 1) * P], early[:, o:o + P],
                                             start=True, stop=True)
                        else:
                            for k in range(LAT):
                                last = pe.matmul(bank[x][:, :], u_sb[:, 1 + k, cc * P:(cc + 1) * P], dft[:, k, x, :],
                                                 start=(k == 0), stop=(k == LAT - 1))
                    last.then_inc(s_f, 1)
                    pe.wait_ge(s_fa, 2 * n + 1)
                    pe.wait_ge(s_fb, n + 1)
                    for x in range(2):
                        last = pe.matmul(bank[2][:, 0:wn], m_cs[:, x, cc, :], y_cs[:, x, 0:wn], start=(x == 0), stop=(x == 1))
                    last.then_inc(s_f, 1)
                    n += 1

            pe.wait_ge(s_qa, T)
            pe.wait_ge(s_qb, T + 1)
            pe.wait_ge(s_cst, 1)
            units = [(i, h) for i in range(T) for h in range(NH)]

            def scores(u):
                i, h = units[u]
                t = turn[i]
                tiles, n_keys = keys_of(t)
                a, b, g = h // 6, (h % 6) // 3, h % 3
                if u >= 3:
                    pe.wait_ge(s_ex, u - 2)
                q = q_t[64 * b:64 * b + 64, t, 3 * a + g, :]
                out = bank[u % 3]
                if t == 0:
                    pe.matmul(out[:, 0:P], q, k_t[64 * b:64 * b + 64, a, 5 * P:6 * P], start=True, stop=True)\
                      .then_inc(s_s, 1)
                    return
                lo, n_win = tiles[0], len(tiles) - 1
                left, right = lo == t - 2, tiles[n_win - 1] == t
                pe.matmul(out[:, 0:n_win * P], q, k_t[64 * b:64 * b + 64, a, lo * P:(lo + n_win) * P],
                          start=True, stop=False)
                if left:
                    pe.matmul(out[:, 0:P], identb[:], maskb[:, 0, :], start=False, stop=not right)
                if right:
                    pe.matmul(out[:, (n_win - 1) * P:n_win * P], identb[:], maskb[:, 1, :], start=False, stop=True)
                pe.matmul(out[:, n_win * P:n_keys], q, k_t[64 * b:64 * b + 64, a, 4 * P:5 * P], start=True, stop=True)\
                  .then_inc(s_s, 1)

            def probs_t(u):
                tiles, n_keys = keys_of(turn[units[u][0]])
                pe.wait_ge(s_ex, u + 1)
                if u >= 2:
                    pe.wait_ge((s_ptb, s_pta)[u % 2], u // 2)
                for m in range(len(tiles)):
                    last = pe.transpose(bank[3 + u % 2][:, m * P:(m + 1) * P], prob[:, u % 2, m * P:(m + 1) * P], ident)
                last.then_inc(s_pt, 1)

            def values(u):
                i, h = units[u]
                tiles, n_keys = keys_of(turn[i])
                n, kv = u // 6, h // 3
                if u % 6 == 0 and n >= 2:
                    pe.wait_ge(s_on, n - 1)
                pe.wait_ge((s_ptb, s_pta)[u % 2], u // 2 + 1)
                for m, kt in enumerate(tiles):
                    vt = {5: 0, 4: T}.get(kt, kt + 1)
                    last = pe.matmul(bank[5 + n % 2][:, (u % 6) * HD:(u % 6 + 1) * HD], prob_t[:, u % 2, m * P:(m + 1) * P],
                                     v_sb[:, vt, kv * HD:(kv + 1) * HD], start=(m == 0), stop=(m == len(tiles) - 1))
                last.then_inc(s_pvu, 1)

            def mix(n):
                pe.wait_ge(s_on, n + 1)
                if n:
                    pe.wait_ge(s_mta, n)
                for m in range(3):
                    last = pe.transpose(bank[7][:, m * P:(m + 1) * P], on[:, n % 2, m * P:(m + 1) * P], ident)
                last.then_inc(s_mt, 1)

            scores(0)
            scores(1)
            pe.wait_ge(s_fa, 8)
            for u in range(len(units)):
                if u + 2 < len(units):
                    scores(u + 2)
                probs_t(u)
                if u:
                    values(u - 1)
                if u % 6 == 3 and u > 6:
                    mix(u // 6 - 1)
            values(len(units) - 1)
            mix(9)

            def spread(n, src):
                pe.wait_ge(s_dg, n + 1)
                if n >= 2:
                    pe.wait_ge(s_ba, n - 1)
                pe.matmul(bank[n % 2][:, :], ones, src.rearrange("p a b -> p (a b)"), start=True, stop=True).then_inc(s_bp, 1)

            for n in range(12):
                spread(n, dg[:, n % 2])

            def out_projection(t, hf):
                if t >= 2:
                    pe.wait_ge(s_x2, 2 * (t - 2) + hf + 1)
                for k in range(KD):
                    w = view(ring, slot(where["wout", k // 4]), 4, D)[:, k % 4, 512 * hf:512 * hf + 512]
                    last = pe.matmul(bank[2 * (t % 2) + hf][:, :], mix_t[:, k, t * P:(t + 1) * P], w,
                                     start=(k == 0), stop=(k == KD - 1))
                last.then_inc(s_op, 1)

            def h2_t(t):
                pe.wait_ge(s_h2, t + 1)
                if t:
                    pe.wait_ge(s_t2a, t)
                    pe.wait_ge(s_t2b, t)
                v = h2row[:, t % 2, :].rearrange("p (q k) -> p k q", k=KD)
                for k in range(KD):
                    last = pe.transpose(bank[4 + k // 4][:, (k % 4) * P:(k % 4 + 1) * P], v[:, k, :], ident)
                    if k % 4 == 3:
                        last.then_inc(s_t2, 1)

            def router(t):
                pe.wait_ge(s_t2a, t + 1)
                pe.wait_ge(s_t2b, t + 1)
                if t >= 2:
                    pe.wait_ge(s_re, t - 1)
                for k in range(KD):
                    last = pe.matmul(bank[6 + t % 2][:, 0:E], h2t[:, k, t * P:(t + 1) * P], wr[:, k, :],
                                     start=(k == 0), stop=(k == KD - 1))
                last.then_inc(s_r, 1)

            arrived(pe, "wout", 0)
            arrived(pe, "wout", 1)
            pe.wait_ge(s_mta, 10)
            pe.wait_ge(s_ba, 12)
            pe.wait_ge(s_late2, 32)
            for t in range(T):
                out_projection(t, 0)
                if t >= 2:
                    router(t - 2)
                out_projection(t, 1)
                if t:
                    h2_t(t - 1)

            def gate_up(s, out, x_of, ks):
                w = w_gu(s)
                for k in ks:
                    last = pe.matmul(bank[out][:, :], x_of(k), w[:, k], start=(k == 0), stop=(k == KD - 1))
                return last

            def h_transposes(src):
                v = src.rearrange("p (q j) -> p j q", j=2)
                for j in range(2):
                    last = pe.transpose(bank[4][:, j * P:(j + 1) * P], v[:, j, :], ident)
                return last

            def down(s, outs, src):
                w = w_dn(s)
                for hf in range(2):
                    for j in range(2):
                        last = pe.matmul(bank[outs[hf]][:, :], src[:, j * P:(j + 1) * P], w[:, j, 512 * hf:512 * hf + 512],
                                         start=(j == 0), stop=(j == 1))
                return last

            def shared_down(t):
                pe.wait_ge(s_shh, t + 1)
                if t:
                    pe.wait_ge(s_she, t)
                h_transposes(hh[:, t % 2, :]).then_inc(s_sht, 1)
                pe.wait_ge(s_she, t + 1)
                if t:
                    pe.wait_ge(s_sho, t)
                down(item_slot(0), (0, 1), h_t[:, t % 2, :]).then_inc(s_shd, 1)

            def shared_up(t):
                if t >= 2:
                    pe.wait_ge(s_shs, t - 1)
                gate_up(item_slot(0), 2 + t % 2, lambda k: h2t[:, k, t * P:(t + 1) * P], range(KD)).then_inc(s_shg, 1)

            pe.wait_ge(s_ring[item_slot(0)], experts_in(0, item_slot(0)))
            pe.wait_ge(s_x2, 2 * (T - 1))
            pe.wait_ge(s_t2a, 1)
            pe.wait_ge(s_t2b, 1)
            shared_up(0)
            router(T - 2)
            h2_t(T - 1)
            shared_up(1)
            pe.wait_ge(s_x2, 2 * T)
            spread(12, dg2[:, 0])
            spread(13, dg2[:, 1])
            router(T - 1)
            spread(14, dg2[:, 0])
            spread(15, dg2[:, 1])
            shared_up(2)
            pe.wait_ge(s_ba, 16)
            shared_down(0)
            pe.wait_ge(s_mm, T)
            pe.wait_ge(s_re, T)
            for t in range(T):
                for o in range(t + 1):
                    pe.matmul(bank[6][:, t * E:(t + 1) * E], upper[:] if o == t else onesb[:], maskm[:, o, :],
                              start=(o == 0), stop=(o == t))
            for o in range(T):
                last = pe.matmul(bank[7][:, 0:E], onesb[:], maskm[:, o, :], start=(o == 0), stop=(o == T - 1))
            last.then_inc(s_pos, 1)
            shared_up(3)
            for t in range(1, T - 1):
                shared_down(t)
            for t in range(T):
                pe.wait_ge(s_oh, t + 1)
                for k in range(TOPK):
                    last = pe.matmul(bank[6][:, 0:2 * NT], a_oh[t % 2][:, k, :], b_oh[t % 2][:, k].rearrange("p a b -> p (a b)"),
                                     start=(t == 0 and k == 0), stop=(t == T - 1 and k == TOPK - 1))
                last.then_inc(s_tb, 1)
            shared_up(T - 1)
            shared_down(T - 1)

            def block_transposes(b, p, gathered):
                pe.wait_ge(s_xg[p], gathered)
                v = xg[:, p, :].rearrange("p (q k) -> p k q", k=KD)
                for k in range(KD):
                    last = pe.transpose(bank[k // 4][:, (k % 4) * P:(k % 4 + 1) * P], v[:, k, :], ident)
                last.then_inc(s_xt, 1)

            def block_h(cb, p):
                pe.wait_ge(s_h, cb + 1)
                at_least(pe, s_he, cb)
                h_transposes(hh[:, p, :]).then_inc(s_ht, 1)

            def block_down(cb, p, s):
                pe.wait_ge(s_he, cb + 1)
                at_least(pe, s_ya, cb)
                at_least(pe, s_yb, cb)
                down(s, (5, 6), h_t[:, p, :]).then_inc(s_y, 1)

            pe.wait_ge(s_tab, 1)
            pe.wait_ge(s_sho, T)
            block_transposes(0, 0, 16)

            def step(i, j):
                b, p, s = i * 4 + j, j % 2, item_slot(j + 1)
                first = isinstance(b, int) and b == 0
                pe.wait_ge(s_ring[s], 16 * uses[s] + (i + (1 if j < 3 else 2)) * 48)
                pe.wait_ge(s_xa, b + 1)
                pe.wait_ge(s_xb, b + 1)
                at_least(pe, s_h, b - 1)
                gate_up(s, 2 + p, lambda k: xg_t[:, p, k * P:(k + 1) * P], range(0, 4))
                if not first:
                    block_h(b - 1, 1 - p)
                gate_up(s, 2 + p, lambda k: xg_t[:, p, k * P:(k + 1) * P], range(4, 8)).then_inc(s_g, 1)
                block_transposes(b + 1, 1 - p, (i * 2 + (j + 1) // 2 + 1) * 16)
                if not first:
                    block_down(b - 1, 1 - p, item_slot(j))

            pe.wait_ge(s_trip, 1)
            last_p = pe.value_load(trip[0:1, 0:1], min_val=E // 2 - 1, max_val=2 * GROUPS - 1)
            odd = pe.value_load(trip[0:1, 1:2], min_val=0, max_val=1)
            for j in range(4):
                step(0, j)
            with pe.Fori(1, GROUPS) as i:
                for half in range(2):
                    with pe.If(i * 2 + half < last_p + 1):
                        for j in range(2 * half, 2 * half + 2):
                            step(i, j)
            block_h(last_p * 2 + 1, 1)
            with pe.If(odd < 1):
                block_down(last_p * 2 + 1, 1, item_slot(2))
            with pe.If(odd > 0):
                block_down(last_p * 2 + 1, 1, item_slot(4))


_INS = ["x_prompt", "x_sample", "cache_k", "cache_v", "c", "c_ctx", "w_mod", "b_mod", "norm1", "w_in", "w_fourier",
        "sink", "w_out", "norm2", "w_router", "router_bias", "w_gate", "w_up", "w_down", "ws_gate", "ws_up",
        "ws_down", "norm_f"]
_OUTS = [("y_prompt", (1, P, D)), ("y_sample", (1, LAT * P, D)), ("new_k", (1, 1, P, NKV, HD)),
         ("new_v", (1, 1, P, NKV, HD))]


def kernel(**inputs):
    import concourse.bacc as bacc
    from concourse.bass_utils import run_bass_kernel_spmd

    nc = bacc.Bacc("TRN2", target_bir_lowering=False, num_devices=1)
    arrays, args = {}, []
    given = [(n, np.ascontiguousarray(inputs[n])) for n in _INS]
    given += list(zip(("keep_c", "early_c", "dft_c"), shape_constants()))
    for name, a in given:
        arrays[f"in_{name}"] = a
        args.append(nc.dram_tensor(f"in_{name}", a.shape, mybir.dt.from_np(a.dtype), kind="ExternalInput").ap())
    for name, shape in _OUTS:
        args.append(nc.dram_tensor(f"out_{name}", shape, F32, kind="ExternalOutput").ap())
    build(nc, *args)
    r = run_bass_kernel_spmd(nc, [arrays], core_ids=[0])
    return tuple(r.results[0][f"out_{name}"] for name, _ in _OUTS)
```
